# Optimizing a Trainium2 kernel written in Bass

```python
import jax, jax.numpy as jnp
from jax import lax
import numpy as np

D_MODEL = 1024
BATCH = 1
SEQ = 128
DEPTH = 1
DEC_BATCH = 1
DEC_SEQ = 512
PAST_LEN = 128

F32 = jnp.float32
GRID_W = 64
EPS = 1e-6
FNET_W = 256
FNET_GROUPS = 4
LRU_W = 256
LRU_BLOCKS = 4
LRU_CONV = 4
LRU_C = 8.0
SC_W = 256
SC_CONV = 3
MLA_HEADS = 8
Q_LORA = 384
KV_LORA = 256
NOPE = 64
ROPE = 32
V_DIM = 64
QK_DIM = NOPE + ROPE
MLA_OUT = MLA_HEADS * V_DIM
N_FREQ = ROPE // 4
ROPE_BASE = 10000.0
ATTN_SCALE = QK_DIM ** -0.5
Q_BLOCK = 128
N_BRANCH = 4
IN_WIDTHS = (FNET_W, LRU_W, LRU_W, SC_W, SC_W, SC_W, Q_LORA, KV_LORA, ROPE)
D_IN = FNET_W + 2 * LRU_W + 3 * SC_W + Q_LORA + KV_LORA + ROPE
N_GROUPS = 4
EXP_PER_GROUP = 8
N_EXPERTS = N_GROUPS * EXP_PER_GROUP
TOP_K = 2
D_EXPERT = 256

kernel_name = 'hybrid_diffusion_prefix_trunk_step'

def split_points():
    return [int(v) for v in np.cumsum(IN_WIDTHS)[:-1]]

def rmsnorm(x, g):
    xf = x.astype(F32)
    y = xf * lax.rsqrt(jnp.mean(xf * xf, axis=-1, keepdims=True) + EPS)
    return (y * g.astype(F32)).astype(x.dtype)

def adaln(cond, w, b):
    m = jax.nn.silu(cond) @ w + b
    return jnp.split(m, 6, axis=-1)

def dwconv(u, w, pad_left):
    K = w.shape[0]
    L = u.shape[1]
    up = jnp.pad(u, ((0, 0), (pad_left, K - 1 - pad_left), (0, 0)))
    y = up[:, 0:L] * w[0]
    for k in range(1, K):
        y = y + up[:, k:k + L] * w[k]
    return y

def fourier_mix(u):
    B, L, _ = u.shape
    ug = u.astype(F32).reshape(B, L, FNET_GROUPS, FNET_W // FNET_GROUPS)
    y = jnp.fft.fftn(ug, axes=(1, 3), norm='ortho').real
    return y.reshape(B, L, FNET_W).astype(u.dtype)

def blockdiag(x, w, b):
    B, L, _ = x.shape
    xb = x.reshape(B, L, LRU_BLOCKS, LRU_W // LRU_BLOCKS)
    return jnp.einsum('blni,nij->blnj', xb, w).reshape(B, L, LRU_W) + b

def linear_scan(a, b, h0, reverse):
    if h0 is not None:
        idx = -1 if reverse else 0
        b = b.at[:, idx].add(a[:, idx] * h0.astype(F32))

    def comb(lft, rgt):
        return (lft[0] * rgt[0], rgt[0] * lft[1] + rgt[1])

    _, h = lax.associative_scan(comb, (a, b), reverse=reverse, axis=1)
    return h

def rglru_dir(xc, p, d, h0, reverse):
    r = jax.nn.sigmoid(blockdiag(xc, p['lru_wa'][d], p['lru_ba'][d]).astype(F32))
    i = jax.nn.sigmoid(blockdiag(xc, p['lru_wx'][d], p['lru_bx'][d]).astype(F32))
    log_a = -LRU_C * r * jax.nn.softplus(-p['lru_lam'][d].astype(F32))
    a = jnp.exp(log_a)
    b = jnp.sqrt(-jnp.expm1(2.0 * log_a)) * (i * xc.astype(F32))
    return linear_scan(a, b, h0, reverse)

def axial_rope(L):
    t = jnp.arange(L, dtype=jnp.int32)
    rows = (t // GRID_W).astype(F32)
    cols = (t % GRID_W).astype(F32)
    inv = ROPE_BASE ** (-jnp.arange(N_FREQ, dtype=F32) / N_FREQ)
    ang = jnp.concatenate([rows[:, None] * inv, cols[:, None] * inv], axis=-1)
    return jnp.cos(ang)[:, None, :], jnp.sin(ang)[:, None, :]

def rope_tail(x, cos, sin):
    xn, xr = x[..., :NOPE], x[..., NOPE:]
    x1 = xr[..., :ROPE // 2].astype(F32)
    x2 = xr[..., ROPE // 2:].astype(F32)
    rot = jnp.concatenate([x1 * cos - x2 * sin, x1 * sin + x2 * cos], axis=-1).astype(x.dtype)
    return jnp.concatenate([xn, rot], axis=-1)

def mla_kv(ckv, kr, w_kvb, g_kn):
    B, L, _ = ckv.shape
    kv = jnp.einsum('blr,rhe->blhe', ckv, w_kvb)
    k_nope, v = kv[..., :NOPE], kv[..., NOPE:]
    k = jnp.concatenate([k_nope, jnp.broadcast_to(kr[:, :, None, :], (B, L, MLA_HEADS, ROPE))], axis=-1)
    return rmsnorm(k, g_kn), v

def attend(q, k, v):
    s = jnp.einsum('bqhe,bkhe->bhqk', q, k).astype(F32) * ATTN_SCALE
    pr = jax.nn.softmax(s, axis=-1).astype(v.dtype)
    return jnp.einsum('bhqk,bkhv->bqhv', pr, v)

def blocked_attend(q, k, v):
    B, L, H, E = q.shape
    qb = q.reshape(B, L // Q_BLOCK, Q_BLOCK, H, E).transpose(1, 0, 2, 3, 4)
    ob = lax.map(lambda qq: attend(qq, k, v), qb)
    return ob.transpose(1, 0, 2, 3, 4).reshape(B, L, H, v.shape[-1])

def token_mixing(h, p, lru_h0, ctx_ckv, ctx_kr):
    B, L, _ = h.shape
    is_ctx = ctx_ckv is None
    z = h @ p['w_in']
    u_f, x_l, g_l, b_s, c_s, x_s, q_c, kv_c, k_r = jnp.split(z, split_points(), axis=-1)
    y_f = fourier_mix(u_f)
    xc = dwconv(x_l, p['lru_conv'], LRU_CONV // 2)
    h_fw = rglru_dir(xc, p, 0, None if is_ctx else lru_h0[:, 0], False)
    h_bw = rglru_dir(xc, p, 1, None if is_ctx else lru_h0[:, 1], True)
    y_l = (h_fw + h_bw).astype(h.dtype) * jax.nn.gelu(g_l)
    y_s = b_s * dwconv(c_s * x_s, p['sc_conv'], SC_CONV // 2)
    q = jnp.einsum('blr,rhe->blhe', rmsnorm(q_c, p['g_qa']), p['w_qb'])
    q = rmsnorm(q, p['g_qn'])
    ckv = rmsnorm(kv_c, p['g_kva'])
    k, v = mla_kv(ckv, k_r, p['w_kvb'], p['g_kn'])
    if not is_ctx:
        cos, sin = axial_rope(L)
        q = rope_tail(q, cos, sin)
        k = rope_tail(k, cos, sin)
        k_ctx, v_ctx = mla_kv(ctx_ckv, ctx_kr, p['w_kvb'], p['g_kn'])
        k = jnp.concatenate([k, k_ctx], axis=1)
        v = jnp.concatenate([v, v_ctx], axis=1)
    o = blocked_attend(q, k, v).reshape(B, L, MLA_OUT)
    br = jnp.stack([y_f @ p['w_pf'], y_l @ p['w_pl'], y_s @ p['w_ps'], o @ p['w_pm']], axis=2)
    gates = jax.nn.sigmoid(h @ p['w_gate']).reshape(B, L, N_BRANCH, D_MODEL)
    out = jnp.sum(gates * br, axis=2) @ p['w_out']
    if is_ctx:
        fin = jnp.stack([h_fw[:, -1], h_bw[:, 0]], axis=1).astype(h.dtype)
        return out, (ckv, k_r, fin)
    return out, None

def hier_moe(h, p):
    B, L, D = h.shape
    t = h.reshape(B * L, D)
    g_logit = (t @ p['w_gr']).astype(F32) + p['b_gr'].astype(F32)
    g_prob = jax.nn.softmax(g_logit, axis=-1)
    g_sel = jnp.argmax(g_logit, axis=-1)
    g_w = jnp.take_along_axis(g_prob, g_sel[:, None], axis=-1)
    e_logit = ((t @ p['w_er']).astype(F32) + p['b_er'].astype(F32)).reshape(-1, N_GROUPS, EXP_PER_GROUP)
    e_in = jnp.einsum('tge,tg->te', e_logit, jax.nn.one_hot(g_sel, N_GROUPS, dtype=F32))
    top_v, top_i = lax.top_k(e_in, TOP_K)
    top_w = jax.nn.softmax(top_v, axis=-1) * g_w
    eid = g_sel[:, None] * EXP_PER_GROUP + top_i
    combine = jnp.einsum('tk,tke->te', top_w, jax.nn.one_hot(eid, N_EXPERTS, dtype=F32)).astype(h.dtype)
    a = jnp.einsum('td,edf->tef', t, p['w1'])
    u = jnp.einsum('td,edf->tef', t, p['w3'])
    y = jnp.einsum('tef,efd->td', jax.nn.silu(a) * u * combine[:, :, None], p['w2'])
    return y.reshape(B, L, D)

def trunk_layer(x, mod, p, lru_h0, ctx_ckv, ctx_kr):
    sh1, sc1, g1, sh2, sc2, g2 = mod
    h = rmsnorm(x, p['norm1_g']) * (1 + sc1) + sh1
    mix, ctx_state = token_mixing(h, p, lru_h0, ctx_ckv, ctx_kr)
    x = x + g1 * mix
    h = rmsnorm(x, p['norm2_g']) * (1 + sc2) + sh2
    x = x + g2 * hier_moe(h, p)
    return x, ctx_state

def setup_inputs(seed: int = 0) -> dict:
    key = jax.random.key(seed)
    ks = iter(jax.random.split(key, 48))
    D = D_MODEL
    bw = LRU_W // LRU_BLOCKS

    def nrm(shape, scale):
        return jax.random.normal(next(ks), shape, F32) * scale

    def gain(shape):
        return 1.0 + nrm(shape, 0.02)

    inputs = {
        'x_prompt': nrm((BATCH, SEQ, D), 1.0),
        'x_sample': nrm((DEC_BATCH, DEC_SEQ, D), 1.0),
        'cache_ckv': nrm((DEC_BATCH, DEPTH, PAST_LEN, KV_LORA), 1.0),
        'cache_krope': nrm((DEC_BATCH, DEPTH, PAST_LEN, ROPE), 1.0),
        'state_rglru': nrm((DEC_BATCH, DEPTH, 2, LRU_W), 0.5),
        'c': nrm((DEC_BATCH, D), 1.0),
        'c_ctx': nrm((D,), 1.0),
        'norm1_g': gain((DEPTH, D)),
        'norm2_g': gain((DEPTH, D)),
        'w_ada': nrm((DEPTH, D, 6 * D), 0.5 * D ** -0.5),
        'b_ada': nrm((DEPTH, 6 * D), 0.02),
        'w_in': nrm((DEPTH, D, D_IN), D ** -0.5),
        'lru_conv': nrm((DEPTH, LRU_CONV, LRU_W), LRU_CONV ** -0.5),
        'lru_wa': nrm((DEPTH, 2, LRU_BLOCKS, bw, bw), bw ** -0.5),
        'lru_ba': nrm((DEPTH, 2, LRU_W), 0.1),
        'lru_wx': nrm((DEPTH, 2, LRU_BLOCKS, bw, bw), bw ** -0.5),
        'lru_bx': nrm((DEPTH, 2, LRU_W), 0.1),
    }
    a8 = jax.random.uniform(next(ks), (DEPTH, 2, LRU_W), F32, 0.9, 0.999)
    a = a8 ** (1.0 / LRU_C)
    inputs['lru_lam'] = jnp.log(a) - jnp.log1p(-a)
    inputs['sc_conv'] = nrm((DEPTH, SC_CONV, SC_W), SC_CONV ** -0.5)
    inputs['g_qa'] = gain((DEPTH, Q_LORA))
    inputs['w_qb'] = nrm((DEPTH, Q_LORA, MLA_HEADS, QK_DIM), Q_LORA ** -0.5)
    inputs['g_kva'] = gain((DEPTH, KV_LORA))
    inputs['w_kvb'] = nrm((DEPTH, KV_LORA, MLA_HEADS, NOPE + V_DIM), KV_LORA ** -0.5)
    inputs['g_qn'] = gain((DEPTH, QK_DIM))
    inputs['g_kn'] = gain((DEPTH, QK_DIM))
    inputs['w_pf'] = nrm((DEPTH, FNET_W, D), FNET_W ** -0.5)
    inputs['w_pl'] = nrm((DEPTH, LRU_W, D), LRU_W ** -0.5)
    inputs['w_ps'] = nrm((DEPTH, SC_W, D), SC_W ** -0.5)
    inputs['w_pm'] = nrm((DEPTH, MLA_OUT, D), MLA_OUT ** -0.5)
    inputs['w_gate'] = nrm((DEPTH, D, N_BRANCH * D), D ** -0.5)
    inputs['w_out'] = nrm((DEPTH, D, D), D ** -0.5)
    inputs['w_gr'] = nrm((DEPTH, D, N_GROUPS), D ** -0.5)
    inputs['b_gr'] = nrm((DEPTH, N_GROUPS), 0.01)
    inputs['w_er'] = nrm((DEPTH, D, N_EXPERTS), D ** -0.5)
    inputs['b_er'] = nrm((DEPTH, N_EXPERTS), 0.01)
    inputs['w1'] = nrm((DEPTH, N_EXPERTS, D, D_EXPERT), D ** -0.5)
    inputs['w3'] = nrm((DEPTH, N_EXPERTS, D, D_EXPERT), D ** -0.5)
    inputs['w2'] = nrm((DEPTH, N_EXPERTS, D_EXPERT, D), D_EXPERT ** -0.5)
    return inputs

def reference(x_prompt, x_sample, cache_ckv, cache_krope, state_rglru, c, c_ctx,
              norm1_g, norm2_g, w_ada, b_ada, w_in, lru_conv, lru_wa, lru_ba, lru_wx, lru_bx,
              lru_lam, sc_conv, g_qa, w_qb, g_kva, w_kvb, g_qn, g_kn, w_pf, w_pl, w_ps, w_pm,
              w_gate, w_out, w_gr, b_gr, w_er, b_er, w1, w3, w2):
    xp, xs = x_prompt, x_sample
    ckv_list, kr_list, lru_list = [], [], []
    for l in range(DEPTH):
        p = {
            'norm1_g': norm1_g[l], 'norm2_g': norm2_g[l], 'w_in': w_in[l],
            'lru_conv': lru_conv[l], 'lru_wa': lru_wa[l], 'lru_ba': lru_ba[l],
            'lru_wx': lru_wx[l], 'lru_bx': lru_bx[l], 'lru_lam': lru_lam[l],
            'sc_conv': sc_conv[l], 'g_qa': g_qa[l], 'w_qb': w_qb[l], 'g_kva': g_kva[l],
            'w_kvb': w_kvb[l], 'g_qn': g_qn[l], 'g_kn': g_kn[l],
            'w_pf': w_pf[l], 'w_pl': w_pl[l], 'w_ps': w_ps[l], 'w_pm': w_pm[l],
            'w_gate': w_gate[l], 'w_out': w_out[l],
            'w_gr': w_gr[l], 'b_gr': b_gr[l], 'w_er': w_er[l], 'b_er': b_er[l],
            'w1': w1[l], 'w3': w3[l], 'w2': w2[l],
        }
        mod_ctx = adaln(c_ctx, w_ada[l], b_ada[l])
        mod_lat = [m[:, None, :] for m in adaln(c, w_ada[l], b_ada[l])]
        xp, (ckv, kr, fin) = trunk_layer(xp, mod_ctx, p, None, None, None)
        ckv_list.append(ckv)
        kr_list.append(kr)
        lru_list.append(fin)
        xs, _ = trunk_layer(xs, mod_lat, p, state_rglru[:, l], cache_ckv[:, l], cache_krope[:, l])
    new_ckv = jnp.stack(ckv_list, axis=1)
    new_krope = jnp.stack(kr_list, axis=1)
    new_rglru = jnp.stack(lru_list, axis=1)
    return (xp, xs, new_ckv, new_krope, new_rglru)


_drawn_inputs = setup_inputs


def setup_inputs(seed=0):
    import zlib

    import numpy as np

    out = dict(_drawn_inputs(seed))
    spreads = {}
    factors = {'cache_ckv': 8.0,
     'cache_krope': 8.0,
     'norm1_g': 3.028,
     'norm2_g': 4.728,
     'lru_ba': 3.817,
     'g_qa': 8.0,
     'w_qb': 2.879,
     'g_kva': 2.859,
     'g_qn': 8.0,
     'g_kn': 8.0,
     'b_gr': 23.584,
     'b_er': 8.0,
     'lru_bx': 3.122}
    for name, (base, spread) in spreads.items():
        noise = np.random.default_rng([zlib.crc32(name.encode()), seed]).standard_normal(out[name].shape)
        drawn = base * np.exp(spread * noise) if base else spread * noise
        out[name] = __import__('jax').numpy.asarray(drawn.astype(out[name].dtype))
    for name, factor in factors.items():
        out[name] = (out[name] * factor).astype(out[name].dtype)
    return out
```

```python
from contextlib import ExitStack

import numpy as np

import concourse.bass as bass
from concourse import mybir

P = 128
D = 1024
KD = D // P
NLAT = 512
NCTX = 128
NT = NLAT + NCTX
TT = NT // P
LT = NLAT // P
PAST = 128
KEYS = NT + PAST
KT = KEYS // P
H = 8
NOPE, ROPE, VD = 64, 32, 64
QK = NOPE + ROPE
HALF = ROPE // 2
GRID_W = 64
QL, KVL = 384, 256
QKV = QL + KVL + ROPE
CT = (QL + KVL) // P
ATTN_SCALE = float(QK) ** -0.5
EPS = 1e-6
ADA = 6 * D // P
ADA_CHUNKS = 12
NG, NE8, NE = 4, 8, 32
FE = 256
C = 80
NX = (2 * NT - 1) // C
CHUNKS = NE + NX
SLOTS = CHUNKS * C
LOGITS = NG + NE
GELU_C = 0.7978845608028654
GELU_A = 0.044715
LOG1P_TERMS = 9
BIG = 3.0e38

XLAT, XCTX = 2, 2 + NLAT + 3
XW = XCTX + NCTX + 1
SLAT, SCTX = 1, 1 + NLAT + 2
SW = SCTX + NCTX + 1

RING = 4096
EW = KD * 2 * FE + 2 * D
W13 = KD * 2 * FE

F32 = mybir.dt.float32
I32 = mybir.dt.int32
ALU = mybir.AluOpType
ACT = mybir.ActivationFunctionType
AX = mybir.AxisListType


def columns(parts):
    at, where = 0, {}
    for name, width in parts:
        where[name] = (at, at + width)
        at += width
    return where, at


COLS, NCOLS = columns([("b_ada", ADA), ("g1", KD), ("g2", KD), ("conv", 8), ("sc", 6), ("ba", 4), ("bx", 4),
                       ("lam", 4), ("g_qa", 3), ("g_kva", 2), ("h0", 4), ("gq", 1), ("gk", 1)])
CONST, NCONST = columns([("ident", P), ("tri", P), ("cos", LT * HALF), ("sin", LT * HALF), ("rev4", NG),
                         ("rev8", NE8), ("ebase", NE), ("xio", NX), ("tok", TT), ("cs64", 2 * P),
                         ("dftc", 2 * P)])
ROWS, NROWS = columns([("gk", ROPE), ("gq", ROPE), ("br", LOGITS)])
TINY, NTINY = columns([("ss1", TT), ("ss2", TT), ("ssq", 2 * TT), ("sskr", KT), ("rs", 16), ("mhalf", 10),
                       ("sp4", 4), ("nsp4", 4), ("lm", 4), ("lr", 4), ("ls", 4), ("lp", 4), ("lq", 4), ("hb", 8),
                       ("fin", 4), ("gcol", 1), ("mx", 2), ("nmx", 2), ("rsum", 2), ("rinv", 2), ("wt", 2 * TT),
                       ("pause", 4)])

Z_NAMES = ["xl0", "xl1", "c0", "c1", "xs0", "xs1", "gl0", "gl1", "b0", "b1", "uf0", "uf1"]
FRONT = [("ada_a", 1)] + [(f"xt{k}", 1) for k in range(KD)]
FRONT += [(n, 1) for n in ("xl0", "xl1", "c0", "c1", "xs0", "xs1", "gl0", "gl1", "l00r", "l00i", "b0", "l01r", "l01i",
                           "b1", "l10r", "l10i", "uf0", "l11r", "l11i", "uf1",
                           "fa0", "fa1", "fa2", "fa3", "fa4", "fy0", "fy1",
                           "qkv0", "qkv1", "ct0", "qkv2", "ct1", "qkv3", "ct2", "qkv4", "ct3", "ct4",
                           "ada_b", "rt")]
FRONT += [("vk0", 2), ("vk1", 2), ("kt0", 1), ("vk2", 2), ("kt1", 1), ("vk3", 2), ("kt2", 1), ("vk4", 2), ("kt3", 1),
          ("vk5", 2), ("kt4", 1), ("q0", 1), ("kt5", 1), ("q1", 1), ("qt0", 1), ("q2", 1), ("qt1", 1), ("q3", 1),
          ("qt2", 1), ("q4", 1), ("qt3", 1), ("qt4", 1)]
JOB = {n: i for i, (n, _) in enumerate(FRONT)}


def filled_count(name):
    return sum(not n.startswith("ada") for n, _ in FRONT[:JOB[name] + 1])


def drained_count(n):
    return sum(d for i, (_, d) in enumerate(FRONT[:n + 1]) if i % 4 == n % 4)


LAST_IN_SLOT = [drained_count(max(i for i in range(len(FRONT)) if i % 4 == s)) for s in range(4)]

RING_USES = [f"ada{i}" for i in range(4)] + ["win0", "win1", "win2", "dft", "qkvA", "qkvB"]
RING_USES += [f"ada{i}" for i in range(4, ADA_CHUNKS)] + ["wkv", "wq"]
RING_USES += [f"gate{i}" for i in range(KD)] + ["woutA", "woutB"]
USE = {n: i for i, n in enumerate(RING_USES)}
GATE0 = USE["gate0"]

UNITS = [(h, t) for h in range(H) for t in range(TT)]
BRANCH = [(0, 2), (2, 4), (4, 6), (6, 10)]


def build(nc, a, out):
    ctx = ExitStack()
    with ctx:
        def sb(name, n, dt=F32):
            return ctx.enter_context(nc.sbuf_tensor(name, [P, n], dt))

        def sem(name):
            return ctx.enter_context(nc.semaphore(name))

        def view(t, at, *shape):
            v = t[:, at:at + int(np.prod(shape))]
            if len(shape) == 1:
                return v
            names = "abcd"[:len(shape)]
            return v.rearrange(f"p ({' '.join(names)}) -> p {' '.join(names)}",
                               **{x: s for x, s in zip(names[1:], shape[1:])})

        psum = ctx.enter_context(nc.psum_tensor("psum", [P, 4, 1024], F32))

        r_w = sb("r_w", 2 * RING)
        wring = [r_w[:, 0:RING], r_w[:, RING:2 * RING]]
        h2 = view(r_w, 0, TT, D)
        xg = view(r_w, TT * D, 2, D)
        wide = view(r_w, (TT + 2) * D, D)
        yab = view(r_w, 0, 2, 2, D)
        r_h = sb("r_h", KD * NT)
        h1T = view(r_h, 0, KD, NT)
        x1 = view(r_h, 0, TT, D)
        r_a = sb("r_a", H * KEYS)
        xtok = view(r_a, 0, TT, D)
        kT = view(r_a, 0, H, KEYS)
        r_b = sb("r_b", KD * NT)
        qT = view(r_b, 0, H, NT)
        merged = view(r_b, 0, KD, NT)
        h2T = view(r_b, 0, KD, NT)
        y_sb = view(r_b, 0, 2, D)
        xgT = view(r_b, 2 * D, 2, KD, C)
        r_c = sb("r_c", 2 * XW + 2 * SW + 6 * NT)
        xl_pad = view(r_c, 0, 2, XW)
        cs_pad = view(r_c, 2 * XW, 2, SW)
        zoff = 2 * XW + 2 * SW
        gl = view(r_c, zoff, 2, NT)
        c_sb = view(r_c, zoff + 2 * NT, 2, NT)
        b_sb = view(r_c, zoff + 4 * NT, 2, NT)
        prob = view(r_c, 0, 2, NT)
        probT = view(r_c, 2 * NT, 2, NT)
        o_tok = view(r_c, 4 * NT, TT, H * VD)
        wexp = [r_a[:, 0:EW], r_c[:, 0:EW]]
        r_t = sb("r_t", 2 * H * QK)
        uf = view(r_t, 0, 2, NT)
        tokbuf = view(r_t, 0, 2, H, QK)
        hT = view(r_t, 0, 2, 2, C)
        gate_e = view(r_t, 4 * C, 2, C)
        sqbuf = sb("sqbuf", H * QK)
        r_v = sb("r_v", 5 * QKV)
        sqx = view(r_v, 0, D)
        qkv_tok = view(r_v, 0, TT, QKV)
        v_sb = view(r_v, 0, KT, H * VD)
        kr_tok = view(sb("r_kr", KT * ROPE), 0, KT, ROPE)
        kr_rot = view(sb("r_krr", KT * ROPE), 0, KT, ROPE)
        rot = view(sb("r_rot", 4 * P), 0, 4, P)
        ckvT = view(sb("r_ckv", 2 * KEYS), 0, 2, KEYS)
        r_d = sb("r_d", 4 * NT)
        af = view(r_d, 0, TT, 512)
        qcT = view(r_d, 0, 3, NT)
        oT = view(r_d, 0, 4, NT)
        r_y = sb("r_y", 6 * NT)
        yf = view(r_y, 0, 2, NT)
        yl = view(r_y, 2 * NT, 2, NT)
        ys = view(r_y, 4 * NT, 2, NT)
        r_s = sb("r_s", 4 * D)
        lt = view(r_s, 0, 4, NT)
        xc = view(r_s, 4 * NT, 2, NT)
        convt = sqbuf[:, 0:XW]
        wb = view(r_s, 0, 2, 10, P)
        gth = view(r_s, 20 * P, 2, NT)
        acc = view(r_v, 0, NT)
        gtmp = sqbuf[:, 0:NT]
        g1_row, a2_row, b2_row, g2_row = (view(r_y, 0, 2, D), view(r_s, 0, 2, D), view(r_s, 2 * D, 2, D),
                                          view(r_d, 0, 2, D))
        lruw = view(sb("lruw", 8 * P), 0, 8, P)
        w_r = view(sb("w_r", KD * LOGITS), 0, KD, LOGITS)
        cols = sb("cols", NCOLS)
        consts = sb("consts", NCONST)
        rows = sb("rows", NROWS)
        tinys = sb("tinys", NTINY)
        cond = view(sb("cond", 2 * KD), 0, KD, 2)
        scond = view(sb("scond", 2 * KD), 0, KD, 2)
        ada = view(sb("ada", ADA * 2), 0, ADA, 2)
        mod1 = view(sb("mod1", KD * 2), 0, KD, 2)
        rowsrc = view(sb("rowsrc", 8 * KD), 0, 8, KD)
        rowsT = sb("rowsT", P)
        ones = sb("ones", P)
        ints = sb("ints", 3 * TT + NX + 1 + CHUNKS + 3, I32)
        slots = ints[:, 0:2 * TT]
        tok_id = ints[:, 2 * TT:3 * TT]
        xinfo = ints[:, 3 * TT:3 * TT + NX + 1]
        tok0 = 3 * TT + NX + 1
        chunk_tok = ints[:, tok0:tok0 + CHUNKS]
        now_tok = [ints[:, tok0 + CHUNKS + i:tok0 + CHUNKS + i + 1] for i in range(2)]
        xtok_id = ints[:, tok0 + CHUNKS + 2:tok0 + CHUNKS + 3]
        R = {}
        at = 0
        for n, w in (("lg", TT * LOGITS), ("e4", TT * NG), ("q4", TT * NG), ("og", TT * NG), ("mul", TT * NE),
                     ("ein", TT * NE8), ("q8", TT * NE8), ("o1", TT * NE8), ("o2", TT * NE8), ("m1", TT * NE),
                     ("m2", TT * NE), ("msum", TT * NE), ("pre", TT * NE), ("t3", TT * NE), ("gmax", TT),
                     ("gw", TT), ("mm", TT), ("v1", TT), ("v2", TT), ("ed", TT), ("sl", TT), ("n", NE), ("ovn", NE),
                     ("incl", NE), ("db", NE), ("one", NE), ("cmp", NX * NE), ("xe", NX)):
            R[n] = (at, at + w)
            at += w
        assert at <= 5 * QKV

        def r(name):
            return r_v[:, R[name][0]:R[name][1]]

        def r3(name, n):
            return r(name).rearrange("p (t n) -> p t n", n=n)

        def col(name, i=0, n=1):
            return cols[:, COLS[name][0] + i:COLS[name][0] + i + n]

        def const(name):
            return consts[:, CONST[name][0]:CONST[name][1]]

        def row(name):
            return rows[:, ROWS[name][0]:ROWS[name][1]]

        def tiny(name, i=0, n=None):
            lo, hi = TINY[name]
            return tinys[:, lo + i:(lo + i + n) if n else hi]

        def spread(ap, axis, n):
            v = ap.unsqueeze(axis)
            shape = list(v.shape)
            shape[axis] = n
            return v.broadcast_to(shape)

        ident, tri = const("ident"), const("tri")
        ssq = tiny("ssq").rearrange("p (t k) -> p t k", k=2)
        rs = tiny("rs").rearrange("p (b h) -> p b h", b=2)

        rows_d = nc.dram_tensor("rows_scratch", [8, D], F32, kind="Internal").ap()
        h2_d = nc.dram_tensor("h2_scratch", [NT, D], F32, kind="Internal").ap()
        table_d = nc.dram_tensor("table_scratch", [SLOTS, 1], I32, kind="Internal").ap()
        y_d = nc.dram_tensor("y_scratch", [SLOTS, D], F32, kind="Internal").ap()

        loaded = {n: sem("loaded_" + n) for n in ("cond", "cols", "x", "consts", "rows", "lruw", "ckv", "krc", "wr",
                                                  "xres", "g1r", "a2r", "b2r", "g2r")}
        ring_loaded = [sem(f"ring_loaded{i}") for i in range(2)]
        wb_loaded = [sem(f"wb_loaded{i}") for i in range(2)]
        ada_used = sem("ada_used")
        filled = sem("front_filled")
        drained = [sem(f"drained{i}") for i in range(4)]
        s_set = sem("memsets_done")
        s_scond = sem("scond_ready")
        s_aact = sem("early_act")
        s_lam = sem("lam_ready")
        s_sp = sem("sp_ready")
        s_sq1 = sem("x_squares")
        s_rstd1 = sem("rstd1_ready")
        s_xhat = sem("xhat_ready")
        s_mod1 = sem("mod1_ready")
        s_xc = sem("xc_ready")
        s_lact = sem("lru_act")
        s_ldve = sem("lru_dve")
        s_gpoly = sem("gelu_poly")
        s_gtanh = sem("gelu_tanh")
        s_fin = sem("fin_ready")
        s_ysc = sem("ys_conv")
        s_ys = sem("ys_ready")
        s_gelu = sem("gelu_ready")
        s_yl = sem("yl_ready")
        s_ssq = sem("qkv_squares")
        s_rq = sem("qkv_rstd")
        s_qn = sem("qkv_normed")
        s_krr = sem("kr_rotated")
        s_ksq = sem("kr_squares")
        s_kss = sem("head_squares")
        s_krs = sem("head_sums")
        s_hr = sem("head_rstd")
        s_qsc = sem("q_scaled")
        s_tok = sem("tokbuf_ready")
        s_rowsT = sem("rowsT_ready")
        s_rowsd = sem("rows_stored")
        s_S = sem("scores_filled")
        s_nmx = sem("max_ready")
        s_prob = sem("probs_ready")
        s_T = sem("probT_filled")
        s_pT = sem("probT_ready")
        s_V = sem("pv_filled")
        s_o = sem("o_ready")
        s_oT = sem("oT_filled")
        s_oTd = sem("oT_ready")
        s_G = sem("gate_filled")
        s_R = sem("branch_filled")
        s_gth = sem("gate_ready")
        s_mrg = sem("branch_taken")
        s_add = sem("branch_added")
        s_mdone = sem("merged_ready")
        s_wo = sem("wout_filled")
        s_x1 = sem("x1_ready")
        s_sq2 = sem("x1_squares")
        s_r2 = sem("rstd2_ready")
        s_h2 = sem("h2_ready")
        s_h2d = sem("h2_stored")
        s_ht = sem("h2T_filled")
        s_htd = sem("h2T_ready")
        s_lg = sem("logits_filled")
        s_ract = sem("router_exp")
        s_rexp = sem("router_exp_in")
        s_part = sem("router_parts")
        s_onehot = sem("onehot_ready")
        s_pre = sem("prefix_filled")
        s_slot = sem("slots_ready")
        s_yzero = sem("y_zeroed")
        s_tset = sem("table_zeroed")
        s_scat = sem("table_scattered")
        s_now = sem("now_tok_ready")
        s_tab = [sem("table_loaded0"), sem("table_loaded1")]
        w_loaded = [sem(f"w_loaded{i}") for i in range(2)]
        xg_loaded = [sem(f"xg_loaded{i}") for i in range(2)]
        s_xT = sem("xgT_filled")
        s_xTd = sem("xgT_ready")
        s_A = sem("hidden_filled")
        s_eth = sem("expert_tanh")
        s_e1 = sem("expert_gated")
        s_hT = sem("hidden_ready")
        s_Y = sem("y_filled")
        s_ya = sem("y_half_act")
        s_yd = sem("y_half_dve")
        y_stored = [sem(f"y_stored{i}") for i in range(2)]
        yab_loaded = [sem(f"yab_loaded{i}") for i in range(2)]
        s_fo = sem("final_ready")
        s_out = sem("outputs_stored")
        x_idx, x_w, x_in = sem("x_index"), sem("x_weights"), sem("x_tokens")
        x_T, x_Td, x_A, x_th, x_g, x_h = (sem("x_filledT"), sem("x_readyT"), sem("x_hidden"), sem("x_tanh"),
                                          sem("x_gated"), sem("x_hiddenT"))
        x_Y, x_yd, x_st = sem("x_yfilled"), sem("x_ytaken"), sem("x_stored")
        act_step, dve_step, pool_step = sem("act_step"), sem("dve_step"), sem("pool_step")

        def stepper(eng, s):
            n = [0]

            def step(ins):
                n[0] += 1
                ins.then_inc(s, 1)
                eng.wait_ge(s, n[0])
            return step

        def take(eng, name):
            eng.wait_ge(filled, filled_count(name))
            return psum[:, JOB[name] % 4, :]

        def drain(name):
            return drained[JOB[name] % 4]

        def wait_drained(eng, *names):
            for name in names:
                eng.wait_ge(drain(name), drained_count(JOB[name]))

        def ring_wait(eng, name):
            n = USE[name]
            eng.wait_ge(ring_loaded[n % 2], 16 * (n // 2 + 1))
            return wring[n % 2]

        block = ctx.enter_context(nc.Block())

        @block.sync
        def _(sp):
            def load(name, dst, src):
                sp.dma_start(dst, src).then_inc(loaded[name], 16)

            def ring_free(name):
                n = USE[name] - 2
                if n < 0:
                    return
                before = RING_USES[n]
                if before.startswith("ada"):
                    sp.wait_ge(ada_used, int(before[3:]) + 1)
                else:
                    last = {"win0": "c1", "win1": "gl1", "win2": "uf1", "dft": "fy1", "qkvA": "qkv4",
                            "qkvB": "qkv4", "wkv": "vk5", "wq": "q4"}[before]
                    sp.wait_ge(filled, filled_count(last))

            def ring(name, src):
                ring_free(name)
                n = USE[name]
                sp.dma_start(wring[n % 2][:, 0:src.shape[1]], src).then_inc(ring_loaded[n % 2], 16)

            x_dram = a["x"].rearrange("(t p) d -> p t d", p=P)
            for s in (y_stored[0], y_stored[1], x_st):
                sp.sem_inc(s, 16)
            load("cond", cond, a["cond"].rearrange("p (k n) -> p k n", n=2))
            load("cols", cols[:, :], a["cols"])
            load("x", xtok, x_dram)
            ring("ada0", a["w_ada"][0])
            ring("ada1", a["w_ada"][1])
            load("consts", consts[:, :], a["consts"])
            load("rows", rows[:, :], a["rows"])
            load("lruw", lruw, a["lruw"].rearrange("p (k n) -> p k n", k=8))
            load("ckv", ckvT[:, :, NT:KEYS], a["ckv_cache"].rearrange("p (k n) -> p k n", k=2))
            load("krc", kr_tok[:, TT, :], a["kr_cache"])
            load("wr", w_r, a["w_r"].rearrange("p (k n) -> p k n", k=KD))
            ring("ada2", a["w_ada"][2])
            ring("ada3", a["w_ada"][3])
            for i in range(3):
                ring(f"win{i}", a["w_in"][i])
            ring("dft", a["dft"])
            ring("qkvA", a["w_qkv"][0])
            ring("qkvB", a["w_qkv"][1])
            for i in range(4, ADA_CHUNKS):
                ring(f"ada{i}", a["w_ada"][i])
            ring("wkv", a["w_kv"])
            ring("wq", a["w_q"])

            def gate_weights(m, s):
                sp.dma_start(wring[(GATE0 + s) % 2], a["w_gate"][bass.ds(m + s, 1), :, :]
                             .rearrange("a p n -> (a p) n")).then_inc(ring_loaded[(GATE0 + s) % 2], 16)
                sp.dma_start(wb[:, s], a["w_br"][bass.ds(m + s, 1), :, :]
                             .rearrange("a p (k n) -> (a p) k n", k=10)).then_inc(wb_loaded[s], 16)

            sp.wait_ge(s_yl, 2)
            for s in range(2):
                ring_free(f"gate{s}")
                gate_weights(0, s)
            sp.wait_ge(s_fin, 4)
            sp.dma_start(out["rglru"], tiny("fin")).then_inc(s_out, 16)
            wait_drained(sp, "ct4")
            sp.dma_start(out["krope"], kr_tok[:, LT, :]).then_inc(s_out, 16)
            sp.dma_start(out["ckv"].rearrange("p (k t) -> p k t", k=2), ckvT[:, :, NLAT:NT]).then_inc(s_out, 16)
            sp.wait_ge(s_rowsT, 1)
            sp.dma_start(rows_d.rearrange("i (k p) -> (i k) p", p=P), rowsT[0:8 * KD, :]).then_inc(s_rowsd, 16)
            sp.wait_ge(s_oTd, 4)
            for s in range(2):
                sp.dma_start(wexp[s], a["w_e"][s]).then_inc(w_loaded[s], 16)
            with sp.Fori(2, KD - 1, 2) as m:
                for s in range(2):
                    sp.wait_ge(s_R, (m + (s - 1)) * 4)
                    gate_weights(m, s)
            for i in range(2):
                sp.wait_ge(s_R, 4 * (KD - 1 + i))
                n = USE["woutA"] + i
                sp.dma_start(wring[n % 2], a["w_out"][i]).then_inc(ring_loaded[n % 2], 16)
            sp.wait_ge(s_mdone, KD)
            sp.wait_ge(s_rowsd, 16)
            load("xres", x1, x_dram)
            for i, (n, dst) in enumerate((("g1r", g1_row), ("a2r", a2_row), ("b2r", b2_row), ("g2r", g2_row))):
                load(n, dst, rows_d[2 * i:2 * i + 2, :].partition_broadcast(P))
            for t in range(TT):
                sp.wait_ge(s_h2, t + 1)
                sp.dma_start(h2_d[t * P:(t + 1) * P, :], h2[:, t, :]).then_inc(s_h2d, 16)
            sp.wait_ge(s_scat, 16 * 2 * TT)
            sp.dma_start(chunk_tok[0:C, 0:2], table_d.rearrange("(c p) a -> p (c a)", p=C)[:, 0:2],
                         allow_slow_non_contiguous=True) \
                .then_inc(s_tab[0], 16)
            sp.dma_start(chunk_tok[0:C, 2:CHUNKS], table_d.rearrange("(c p) a -> p (c a)", p=C)[:, 2:CHUNKS],
                         allow_slow_non_contiguous=True) \
                .then_inc(s_tab[1], 16)

            def store_y(c, s):
                sp.wait_ge(s_ya, c + (s + 3))
                sp.wait_ge(s_yd, c + (s + 3))
                sp.dma_start(y_d.rearrange("(c p) d -> c p d", p=C)[bass.ds(c + s, 1), :, :]
                             .rearrange("a p d -> (a p) d"), y_sb[0:C, s, :]).then_inc(y_stored[s], 16)

            with sp.Fori(0, NE - 3, 2) as c:
                for s in range(2):
                    sp.wait_ge(s_Y, c + (s + 1))
                    sp.dma_start(wexp[s], a["w_e"][bass.ds(c + (s + 2), 1), :, :]
                                 .rearrange("a p n -> (a p) n")).then_inc(w_loaded[s], 16)
                    store_y(c, s)
            for s in range(2):
                store_y(NE - 2, s)
            sp.wait_ge(s_slot, 2)
            n_x = sp.value_load(xinfo[0:1, NX:NX + 1], min_val=0, max_val=NX)
            with sp.Fori(0, NX) as x:
                with sp.If(x < n_x):
                    sp.wait_ge(x_st, (x + 1) * 16)
                    sp.wait_ge(s_yzero, 16)
                    e = sp.value_load(xinfo[0:1, bass.ds(x, 1)], min_val=0, max_val=NE - 1)
                    sp.dma_start(wexp[0], a["w_e"][bass.ds(e, 1), :, :].rearrange("a p n -> (a p) n")) \
                        .then_inc(x_w, 16)
                    sp.dma_start(xtok_id[0:C, :], table_d.rearrange("(c p) a -> c p a", p=C)
                                 [bass.ds(x + NE, 1), :, :].rearrange("a p b -> (a p) b")).then_inc(x_idx, 16)
                    sp.wait_ge(x_yd, x + 1)
                    sp.dma_start(y_d.rearrange("(c p) d -> c p d", p=C)[bass.ds(x + NE, 1), :, :]
                                 .rearrange("a p d -> (a p) d"), y_sb[0:C, 0, :]).then_inc(x_st, 16)
            for t in range(TT):
                sp.wait_ge(s_fo, t + 1)
                sp.dma_start(out["y"][t * P:(t + 1) * P, :], x1[:, t, :]).then_inc(s_out, 16)
            sp.wait_ge(s_out, 16 * (3 + TT))

        @block.tensor
        def _(pe):
            mm, flip = nc.tensor.matmul, nc.tensor.transpose

            def begin(name):
                n = JOB[name]
                if n >= 4:
                    pe.wait_ge(drained[n % 4], drained_count(n - 4))
                return psum[:, n % 4, :]

            def both(o, w, x, **flags):
                mm(o[:, 0:NLAT], w, x[:, 0:NLAT], **flags)
                return mm(o[:, NLAT:NT], w, x[:, NLAT:NT], **flags)

            def modulation(o, first, last):
                for ch in range(first, last):
                    w = ring_wait(pe, f"ada{ch}").rearrange("p (k n) -> p k n", k=KD)
                    for j in range(4):
                        m = (ch - first) * 4 + j
                        for k in range(KD):
                            ins = mm(o[:, 2 * m:2 * m + 2], w[:, k, j * P:(j + 1) * P], scond[:, k, :],
                                     start=(k == 0), stop=(k == KD - 1))
                    ins.then_inc(ada_used, 1)

            o = begin("ada_a")
            pe.wait_ge(s_scond, 1)
            modulation(o, 0, 4)

            pe.wait_ge(loaded["consts"], 16)
            pe.wait_ge(s_xhat, TT)
            for k in range(KD):
                o = begin(f"xt{k}")
                for t in range(TT):
                    ins = flip(o[:, t * P:(t + 1) * P], xtok[:, t, k * P:(k + 1) * P], ident)
                ins.then_inc(filled, 1)

            def wide_z(name):
                i = Z_NAMES.index(name)
                w = ring_wait(pe, f"win{i // 4}").rearrange("p (j k n) -> p j k n", j=4, k=KD)
                o = begin(name)
                for k in range(KD):
                    ins = both(o, w[:, i % 4, k, :], h1T[:, k, :], start=(k == 0), stop=(k == KD - 1))
                ins.then_inc(filled, 1)

            def lru_gates(d, j):
                for x in range(2):
                    o = begin(f"l{d}{j}{'ri'[x]}")
                    pe.wait_ge(loaded["lruw"], 16)
                    pe.wait_ge(s_xc, j + 1)
                    both(o, lruw[:, (d * 2 + x) * 2 + j, :], xc[:, j, :], start=True, stop=True).then_inc(filled, 1)

            wait_drained(pe, *[f"xt{k}" for k in range(KD)])
            for n in Z_NAMES[:8]:
                wide_z(n)
            lru_gates(0, 0)
            wide_z("b0")
            lru_gates(0, 1)
            wide_z("b1")
            lru_gates(1, 0)
            wide_z("uf0")
            lru_gates(1, 1)
            wide_z("uf1")

            wait_drained(pe, "uf0", "uf1")
            for t in range(TT):
                o = begin(f"fa{t}")
                for j in range(2):
                    ins = mm(o[:, j * 256:(j + 1) * 256], uf[:, j, t * P:(t + 1) * P], const("cs64"),
                             start=True, stop=True)
                ins.then_inc(filled, 1)
            wait_drained(pe, *[f"fa{t}" for t in range(TT)])
            w = ring_wait(pe, "dft").rearrange("p (t s n) -> p t s n", t=LT, s=2)
            wc = const("dftc").rearrange("p (s n) -> p s n", s=2)
            for j in range(2):
                o = begin(f"fy{j}")
                for t in range(LT):
                    for s in range(2):
                        mm(o[:, 0:NLAT], af[:, t, j * 256 + s * P:j * 256 + (s + 1) * P], w[:, t, s, :],
                           start=(t == 0 and s == 0), stop=(t == LT - 1 and s == 1))
                for s in range(2):
                    ins = mm(o[:, NLAT:NT], af[:, LT, j * 256 + s * P:j * 256 + (s + 1) * P], wc[:, s, :],
                             start=(s == 0), stop=(s == 1))
                ins.then_inc(filled, 1)

            def qkv(t):
                o = begin(f"qkv{t}")
                for k in range(KD):
                    w = ring_wait(pe, "qkvA" if k < 4 else "qkvB")[:, (k % 4) * QKV:(k % 4 + 1) * QKV]
                    x = h1T[:, k, t * P:(t + 1) * P]
                    mm(o[:, 0:512], x, w[:, 0:512], start=(k == 0), stop=(k == KD - 1))
                    ins = mm(o[:, 512:QKV], x, w[:, 512:QKV], start=(k == 0), stop=(k == KD - 1))
                ins.then_inc(filled, 1)

            def latents_T(t):
                o = begin(f"ct{t}")
                pe.wait_ge(s_qn, t + 1)
                for i in range(CT):
                    ins = flip(o[:, i * P:(i + 1) * P], qkv_tok[:, t, i * P:(i + 1) * P], ident)
                ins.then_inc(filled, 1)

            qkv(0)
            for t in range(1, TT):
                qkv(t)
                latents_T(t - 1)
            latents_T(TT - 1)

            o = begin("ada_b")
            modulation(o, 4, ADA_CHUNKS)
            o = begin("rt")
            pe.wait_ge(s_mod1, 2)
            flip(o[0:8 * KD, 0:P], rowsrc.rearrange("p i k -> p (i k)"), ident).then_inc(filled, 1)

            def keys_values(t):
                o = begin(f"vk{t}")
                if t == 0:
                    wait_drained(pe, *[f"ct{u}" for u in range(TT)])
                    pe.wait_ge(loaded["ckv"], 16)
                w = ring_wait(pe, "wkv")[:, 0:2 * D].rearrange("p (k n) -> p k n", k=2)
                for k in range(2):
                    for n in range(2):
                        ins = mm(o[:, n * 512:(n + 1) * 512], ckvT[:, k, t * P:(t + 1) * P],
                                 w[:, k, n * 512:(n + 1) * 512], start=(k == 0), stop=(k == 1))
                ins.then_inc(filled, 1)

            def queries(t):
                o = begin(f"q{t}")
                w = ring_wait(pe, "wq")[:, 0:3 * H * QK].rearrange("p (k n) -> p k n", k=3)
                for k in range(3):
                    x = qcT[:, k, t * P:(t + 1) * P]
                    mm(o[:, 0:512], x, w[:, k, 0:512], start=(k == 0), stop=(k == 2))
                    ins = mm(o[:, 512:H * QK], x, w[:, k, 512:H * QK], start=(k == 0), stop=(k == 2))
                ins.then_inc(filled, 1)

            def heads_T(name, n):
                o = begin(name)
                pe.wait_ge(s_tok, n + 1)
                for h in range(H):
                    ins = flip(o[0:QK, h * P:(h + 1) * P], tokbuf[:, n % 2, h, :], ident)
                ins.then_inc(filled, 1)

            keys_values(0)
            for t in range(1, KT):
                keys_values(t)
                heads_T(f"kt{t - 1}", t - 1)
            queries(0)
            heads_T("kt5", KT - 1)
            for t in range(1, TT):
                queries(t)
                heads_T(f"qt{t - 1}", KT + t - 1)
            heads_T("qt4", KT + TT - 1)

            for s in range(4):
                pe.wait_ge(drained[s], LAST_IN_SLOT[s])

            def scores(i):
                h, t = UNITS[i]
                if i >= 2:
                    pe.wait_ge(s_prob, i - 1)
                q, o = qT[0:QK, h, t * P:(t + 1) * P], psum[:, i % 2, :]
                if t < LT:
                    mm(o[:, 0:512], q, kT[0:QK, h, 0:NLAT], start=True, stop=True)
                    ins = mm(o[:, 512:640], q, kT[0:QK, h, NT:KEYS], start=True, stop=True)
                else:
                    ins = mm(o[:, 0:P], q, kT[0:QK, h, NLAT:NT], start=True, stop=True)
                ins.then_inc(s_S, 1)

            scores(0)
            scores(1)
            for i, (h, t) in enumerate(UNITS):
                keys = [0, 1, 2, 3, 5] if t < LT else [4]
                pe.wait_ge(s_prob, i + 1)
                if i >= 1:
                    pe.wait_ge(s_pT, i)
                for j in range(len(keys)):
                    ins = flip(psum[:, 2, j * P:(j + 1) * P], prob[:, i % 2, j * P:(j + 1) * P], ident)
                ins.then_inc(s_T, 1)
                if i + 2 < len(UNITS):
                    scores(i + 2)
                pe.wait_ge(s_pT, i + 1)
                if i >= 2:
                    pe.wait_ge(s_o, i - 1)
                for j, kt in enumerate(keys):
                    ins = mm(psum[:, 3, (i % 2) * 512:(i % 2) * 512 + VD], probT[:, i % 2, j * P:(j + 1) * P],
                             v_sb[:, kt, h * VD:(h + 1) * VD], start=(j == 0), stop=(j == len(keys) - 1))
                ins.then_inc(s_V, 1)

            pe.wait_ge(s_o, len(UNITS))
            for p in range(4):
                for t in range(TT):
                    ins = flip(psum[:, p, t * P:(t + 1) * P], o_tok[:, t, p * P:(p + 1) * P], ident)
                ins.then_inc(s_oT, 1)

            pe.wait_ge(s_oTd, 4)
            pe.wait_ge(s_yl, 2)
            pe.wait_ge(s_ys, 2)
            inputs = [yf[:, 0], yf[:, 1], yl[:, 0], yl[:, 1], ys[:, 0], ys[:, 1]] + [oT[:, i] for i in range(4)]
            with pe.Fori(0, KD - 1, 2) as m:
                for s in range(2):
                    pe.wait_ge(ring_loaded[(GATE0 + s) % 2], m * 8 + 16 * ((GATE0 + s) // 2 + 1))
                    pe.wait_ge(wb_loaded[s], m * 8 + 16)
                    w = wring[(GATE0 + s) % 2].rearrange("p (b k n) -> p b k n", b=4, k=KD)
                    for b, (lo, hi) in enumerate(BRANCH):
                        og, ob = psum[:, (2 * b) % 4, :], psum[:, (2 * b + 1) % 4, :]
                        pe.wait_ge(s_gth, m * 4 + (4 * s + b + 1))
                        for k in range(KD):
                            ins = both(og, w[:, b, k, :], h1T[:, k, :], start=(k == 0), stop=(k == KD - 1))
                        ins.then_inc(s_G, 1)
                        pe.wait_ge(s_mrg, m * 4 + (4 * s + b + 1))
                        for kk in range(lo, hi):
                            ins = both(ob, wb[:, s, kk, :], inputs[kk], start=(kk == lo), stop=(kk == hi - 1))
                        ins.then_inc(s_R, 1)

            wo = [ring_wait(pe, "woutA"), ring_wait(pe, "woutB")]
            pe.wait_ge(s_mdone, KD)
            pe.wait_ge(s_gth, 4 * KD + 2)
            for t in range(TT):
                if t >= 2:
                    pe.wait_ge(s_x1, t - 1)
                for k in range(KD):
                    for n in range(2):
                        ins = mm(psum[:, t % 2, n * 512:(n + 1) * 512], merged[:, k, t * P:(t + 1) * P],
                                 wo[k // 4][:, (k % 4) * D + n * 512:(k % 4) * D + (n + 1) * 512],
                                 start=(k == 0), stop=(k == KD - 1))
                ins.then_inc(s_wo, 1)
            for t in range(TT):
                pe.wait_ge(s_h2, t + 1)
                if t >= 2:
                    pe.wait_ge(s_htd, t - 1)
                for k in range(KD):
                    ins = flip(psum[:, 2 + t % 2, k * P:(k + 1) * P], h2[:, t, k * P:(k + 1) * P], ident)
                ins.then_inc(s_ht, 1)
            pe.wait_ge(s_htd, TT)
            pe.wait_ge(loaded["wr"], 16)
            for t in range(TT):
                for k in range(KD):
                    ins = mm(psum[:, 0, t * LOGITS:(t + 1) * LOGITS], h2T[:, k, t * P:(t + 1) * P], w_r[:, k, :],
                             start=(k == 0), stop=(k == KD - 1))
            ins.then_inc(s_lg, 1)
            pe.wait_ge(s_onehot, 1)
            msum = r3("msum", NE)
            for t in range(TT + 1):
                for u in range(min(t + 1, TT)):
                    ins = mm(psum[:, 1, t * NE:(t + 1) * NE], tri if u == t else ones[:, :], msum[:, u, :],
                             start=(u == 0), stop=(u == min(t, TT - 1)))
            ins.then_inc(s_pre, 1)

            def hidden(w, s):
                wv = w[:, 0:W13].rearrange("p (k n) -> p k n", k=KD)
                for f in range(4):
                    for k in range(KD):
                        ins = mm(psum[:, 1, f * C:(f + 1) * C], wv[:, k, f * P:(f + 1) * P], xgT[:, s, k, :],
                                 start=(k == 0), stop=(k == KD - 1))
                return ins

            def project(w, s, y):
                w2 = w[:, W13:EW].rearrange("p (k n) -> p k n", k=2)
                for k in range(2):
                    for n in range(2):
                        ins = mm(y[0:C, n * 512:(n + 1) * 512], hT[:, s, k, :], w2[:, k, n * 512:(n + 1) * 512],
                                 start=(k == 0), stop=(k == 1))
                return ins

            def chunk_T(s):
                for k in range(KD):
                    ins = flip(psum[:, 0, k * P:k * P + C], xg[0:C, s, k * P:(k + 1) * P], ident[0:C, 0:C])
                return ins

            pe.wait_ge(s_slot, 2)
            pe.wait_ge(xg_loaded[0], 16)
            chunk_T(0).then_inc(s_xT, 1)
            with pe.Fori(0, NE - 1, 2) as c:
                for s in range(2):
                    pe.wait_ge(w_loaded[s], c * 8 + 16)
                    pe.wait_ge(s_xTd, c + (s + 1))
                    hidden(wexp[s], s).then_inc(s_A, 1)
                    pe.wait_ge(xg_loaded[1 - s], c * 8 + 16 * (s + 1))
                    chunk_T(1 - s).then_inc(s_xT, 1)
                    pe.wait_ge(s_hT, c + (s + 1))
                    pe.wait_ge(s_ya, c + (s + 1))
                    pe.wait_ge(s_yd, c + (s + 1))
                    project(wexp[s], s, psum[:, 2 + s, :]).then_inc(s_Y, 1)
            pe.wait_ge(s_ya, NE + 2)
            pe.wait_ge(s_yd, NE + 2)
            pe.wait_ge(s_xTd, NE + 1)
            n_x = pe.value_load(xinfo[0:1, NX:NX + 1], min_val=0, max_val=NX)
            with pe.Fori(0, NX) as x:
                with pe.If(x < n_x):
                    pe.wait_ge(x_in, (x + 1) * 16)
                    chunk_T(0).then_inc(x_T, 1)
                    pe.wait_ge(x_Td, x + 1)
                    pe.wait_ge(x_w, (x + 1) * 16)
                    hidden(wexp[0], 0).then_inc(x_A, 1)
                    pe.wait_ge(x_h, x + 1)
                    project(wexp[0], 0, psum[:, 2, :]).then_inc(x_Y, 1)

        @block.scalar
        def _(act):
            step = stepper(act, act_step)
            A = nc.scalar.activation

            act.wait_ge(loaded["cond"], 16)
            A(scond, cond, ACT.Tanh, scale=0.5).then_inc(s_aact, 1)
            act.wait_ge(s_lam, 1)
            A(tiny("lr"), tiny("lm"), ACT.Exp, scale=-1.0).then_inc(s_aact, 1)
            act.wait_ge(loaded["x"], 16)
            for t in range(TT):
                if t:
                    act.wait_ge(s_sq1, t)
                A(sqx, xtok[:, t, :], ACT.Square, scale=D ** -0.5, accum_out=tiny("ss1", t, 1)).then_inc(s_sq1, 1)

            act.wait_ge(s_mod1, 1)
            for k in range(0, KD, 2):
                o = take(act, f"xt{k}")
                A(h1T[:, k, 0:NLAT], o[:, 0:NLAT], ACT.Identity, bias=ada[:, k, 0:1], scale=mod1[:, k, 0:1])
                A(h1T[:, k, NLAT:NT], o[:, NLAT:NT], ACT.Identity, bias=ada[:, k, 1:2],
                  scale=mod1[:, k, 1:2]).then_inc(drain(f"xt{k}"), 1)

            def copy_z(n):
                o = take(act, n)
                kind, j = n[:-1], int(n[-1])
                if kind == "xl":
                    A(xl_pad[:, j, XLAT:XLAT + NLAT], o[:, 0:NLAT], ACT.Copy)
                    A(xl_pad[:, j, XCTX:XCTX + NCTX], o[:, NLAT:NT], ACT.Copy).then_inc(drain(n), 1)
                    return
                if kind == "gl":
                    A(yf[:, j, :], o[:, 0:NT], ACT.Square)
                A({"gl": gl, "c": c_sb, "b": b_sb, "uf": uf}[kind][:, j, :], o[:, 0:NT], ACT.Copy) \
                    .then_inc(drain(n), 1)

            def lru_act(n):
                d, j = divmod(n, 2)
                if n >= 1:
                    act.wait_ge(s_ldve, 3 * n)
                o = take(act, f"l{d}{j}r")
                A(lt[:, 0, :], o[:, 0:NT], ACT.Tanh, bias=tiny("hb", n, 1), scale=0.5) \
                    .then_inc(drain(f"l{d}{j}r"), 1)
                o = take(act, f"l{d}{j}i")
                A(lt[:, 1, :], o[:, 0:NT], ACT.Tanh, bias=tiny("hb", 4 + n, 1), scale=0.5) \
                    .then_inc(drain(f"l{d}{j}i"), 1)
                wait_drained(act, f"l{d}{j}r")
                step(A(lt[:, 2, :], lt[:, 0, :], ACT.Exp, bias=tiny("nsp4", n, 1), scale=tiny("nsp4", n, 1)))
                A(lt[:, 0, :], lt[:, 0, :], ACT.Tanh, bias=tiny("sp4", n, 1), scale=tiny("sp4", n, 1))
                A(lt[:, 3, :], lt[:, 2, :], ACT.Square).then_inc(s_lact, 1)

            def lru_root(n):
                act.wait_ge(s_ldve, 3 * n + 1)
                A(lt[:, 3, :], lt[:, 3, :], ACT.Sqrt, scale=0.25).then_inc(s_lact, 1)

            act.wait_ge(s_set, 4)
            for n in ("xl0", "xl1", "c0", "c1", "gl0", "gl1"):
                copy_z(n)
            act.wait_ge(s_sp, 1)
            lru_act(0)
            copy_z("b0")
            lru_root(0)
            for j in range(2):
                act.wait_ge(s_gpoly, j + 1)
                A(yf[:, j, :], yf[:, j, :], ACT.Tanh, scale=GELU_C).then_inc(s_gtanh, 1)
            lru_act(1)
            copy_z("b1")
            lru_root(1)
            lru_act(2)
            copy_z("uf0")
            lru_root(2)
            lru_act(3)
            copy_z("uf1")
            lru_root(3)

            for t in range(TT):
                o = take(act, f"qkv{t}")
                if t:
                    act.wait_ge(s_ssq, t)
                A(sqbuf[:, 0:QL], o[:, 0:QL], ACT.Square, scale=QL ** -0.5, accum_out=ssq[:, t, 0:1])
                A(sqbuf[:, QL:QL + KVL], o[:, QL:QL + KVL], ACT.Square, scale=KVL ** -0.5,
                  accum_out=ssq[:, t, 1:2]).then_inc(s_ssq, 1)

            def keys_act(t):
                o = take(act, f"vk{t}")
                if t:
                    act.wait_ge(s_krs, t)
                A(sqbuf[:, 0:H * NOPE], o[:, 0:H * NOPE], ACT.Square).then_inc(s_kss, 1)
                A(v_sb[:, t, :], o[:, 512:1024], ACT.Copy).then_inc(drain(f"vk{t}"), 1)

            def keys_T(t):
                o = take(act, f"kt{t}")
                A(kT[0:QK, :, t * P:(t + 1) * P], o[0:QK, :].rearrange("p (h n) -> p h n", h=H), ACT.Copy) \
                    .then_inc(drain(f"kt{t}"), 1)

            def queries_act(t):
                o = take(act, f"q{t}")
                act.wait_ge(s_krs, KT + t)
                A(sqbuf[:, :], o[:, 0:H * QK], ACT.Square).then_inc(s_kss, 1)

            wait_drained(act, "ct4")
            keys_act(0)
            for t in range(1, KT):
                keys_act(t)
                keys_T(t - 1)
            queries_act(0)
            keys_T(KT - 1)
            for t in range(1, TT):
                queries_act(t)

            def exps(i):
                w = NT if UNITS[i][1] < LT else P
                act.wait_ge(s_nmx, i + 1)
                if i >= 2:
                    act.wait_ge(s_T, i - 1)
                    act.wait_ge(s_o, i - 1)
                A(prob[:, i % 2, 0:w], psum[:, i % 2, 0:w], ACT.Exp, bias=tiny("nmx", i % 2, 1), scale=ATTN_SCALE,
                  accum_out=tiny("rsum", i % 2, 1)).then_inc(s_prob, 1)

            exps(0)
            exps(1)
            for i in range(len(UNITS)):
                if i % 2:
                    w = NT if UNITS[i][1] < LT else P
                    act.wait_ge(s_T, i + 1)
                    if i >= 2:
                        act.wait_ge(s_V, i - 1)
                    A(probT[:, 1, 0:w], psum[:, 2, 0:w], ACT.Copy).then_inc(s_pT, 1)
                if i + 2 < len(UNITS):
                    exps(i + 2)
            for p in (0, 2):
                act.wait_ge(s_oT, p + 1)
                A(oT[:, p, :], psum[:, p, 0:NT], ACT.Copy).then_inc(s_oTd, 1)

            act.sem_inc(s_gth, 2)
            with act.Fori(0, KD - 1, 2) as m:
                for g in range(8):
                    act.wait_ge(s_G, m * 4 + (g + 1))
                    act.wait_ge(s_mrg, m * 4 + (g + 1))
                    A(gth[:, g % 2, :], psum[:, (2 * g) % 4, 0:NT], ACT.Tanh, scale=0.5).then_inc(s_gth, 1)

            for t in range(TT):
                act.wait_ge(s_x1, t + 1)
                if t:
                    act.wait_ge(s_sq2, t)
                A(view(r_t, 0, D), x1[:, t, :], ACT.Square, scale=D ** -0.5,
                  accum_out=tiny("ss2", t, 1)).then_inc(s_sq2, 1)
            for t in range(TT):
                act.wait_ge(s_ht, t + 1)
                A(h2T[:, :, t * P:(t + 1) * P], psum[:, 2 + t % 2, :].rearrange("p (k n) -> p k n", k=KD), ACT.Copy) \
                    .then_inc(s_htd, 1)
            act.wait_ge(s_rexp, 1)
            A(r("e4"), r("e4"), ACT.Exp).then_inc(s_ract, 1)
            act.wait_ge(s_rexp, 2)
            A(r("ed"), r("ed"), ACT.Exp).then_inc(s_ract, 1)

            act.wait_ge(s_slot, 2)
            act.sem_inc(s_ya, 2)

            def take_T(s, done):
                A(xgT[:, s, :, :], psum[:, 0, :].rearrange("p (k n) -> p k n", k=KD)[:, :, 0:C], ACT.Copy) \
                    .then_inc(done, 1)

            def tanh_a(done):
                A(gate_e, psum[:, 1, 0:2 * C].rearrange("p (f n) -> p f n", f=2), ACT.Tanh, scale=0.5) \
                    .then_inc(done, 1)

            act.wait_ge(s_xT, 1)
            take_T(0, s_xTd)
            with act.Fori(0, NE - 1, 2) as c:
                for s in range(2):
                    act.wait_ge(s_A, c + (s + 1))
                    tanh_a(s_eth)
                    act.wait_ge(s_xT, c + (s + 2))
                    take_T(1 - s, s_xTd)
                    act.wait_ge(s_Y, c + (s + 1))
                    act.wait_ge(y_stored[s], c * 8 + 16)
                    A(y_sb[0:C, s, 0:512], psum[0:C, 2 + s, 0:512], ACT.Copy).then_inc(s_ya, 1)
            for s in range(2):
                act.wait_ge(y_stored[s], 8 * NE + 16)
            n_x = act.value_load(xinfo[0:1, NX:NX + 1], min_val=0, max_val=NX)
            with act.Fori(0, NX) as x:
                with act.If(x < n_x):
                    act.wait_ge(x_T, x + 1)
                    take_T(0, x_Td)
                    act.wait_ge(x_A, x + 1)
                    tanh_a(x_th)
                    act.wait_ge(x_Y, x + 1)
                    A(y_sb[0:C, 0, :], psum[0:C, 2, :], ACT.Copy).then_inc(x_yd, 1)

        @block.vector
        def _(dve):
            v = nc.vector
            step = stepper(dve, dve_step)

            v.memset(ones[:, :], 1.0).then_inc(s_set, 1)
            v.memset(r_c[:, 0:2 * XW + 2 * SW], 0.0).then_inc(s_set, 1)
            v.memset(tiny("gcol"), 1.0).then_inc(s_set, 1)
            v.memset(tiny("mhalf"), -0.5).then_inc(s_set, 1)
            dve.wait_ge(s_aact, 1)
            dve.wait_ge(loaded["cond"], 16)
            step(v.scalar_tensor_tensor(out=scond, in0=scond, scalar=1.0, in1=cond, op0=ALU.add, op1=ALU.mult))
            v.tensor_scalar(scond, scond, 0.5, None, ALU.mult).then_inc(s_scond, 1)
            dve.wait_ge(loaded["cols"], 16)
            lam = col("lam", 0, 4)
            step(v.tensor_scalar(tiny("lm"), lam, -1.0, None, ALU.mult))
            step(v.tensor_tensor(tiny("lp"), tiny("lm"), lam, ALU.max))
            step(v.tensor_copy(tiny("ls"), tiny("lm")))
            v.tensor_copy(tiny("lm"), tiny("lp")).then_inc(s_lam, 1)
            step(v.tensor_scalar(tiny("lq"), tiny("ls"), 0.0, 4.0, ALU.max, ALU.mult))
            step(v.tensor_copy(tiny("sp4"), tiny("lq")))
            dve.wait_ge(s_aact, 2)
            step(v.tensor_scalar(tiny("lp"), tiny("lr"), 2.0, None, ALU.add))
            step(v.reciprocal(tiny("ls"), tiny("lp")))
            step(v.tensor_tensor(tiny("ls"), tiny("ls"), tiny("lr"), ALU.mult))
            step(v.tensor_tensor(tiny("lp"), tiny("ls"), tiny("ls"), ALU.mult))
            step(v.tensor_scalar(tiny("lq"), tiny("lp"), 1.0 / (2 * LOG1P_TERMS + 1), None, ALU.mult))
            for k in range(LOG1P_TERMS - 1, 0, -1):
                step(v.scalar_tensor_tensor(out=tiny("lq"), in0=tiny("lq"), scalar=1.0 / (2 * k + 1), in1=tiny("lp"),
                                            op0=ALU.add, op1=ALU.mult))
            step(v.scalar_tensor_tensor(out=tiny("lq"), in0=tiny("lq"), scalar=1.0, in1=tiny("ls"),
                                        op0=ALU.add, op1=ALU.mult))
            step(v.scalar_tensor_tensor(out=tiny("sp4"), in0=tiny("lq"), scalar=8.0, in1=tiny("sp4"),
                                        op0=ALU.mult, op1=ALU.add))
            v.tensor_scalar(tiny("nsp4"), tiny("sp4"), -1.0, None, ALU.mult)
            v.tensor_scalar(tiny("hb"), col("ba", 0, 8), 0.5, None, ALU.mult).then_inc(s_sp, 1)
            dve.wait_ge(s_set, 4)
            v.tensor_tensor(tiny("gcol")[0:NOPE, :], col("gq")[0:NOPE, :], col("gk")[0:NOPE, :], ALU.mult)

            dve.wait_ge(s_rstd1, 1)
            for t in range(TT):
                v.tensor_scalar(xtok[:, t, :], xtok[:, t, :], tiny("ss1", t, 1), None, ALU.mult).then_inc(s_xhat, 1)

            def take_modulation(name, first, n, used):
                dve.wait_ge(ada_used, used)
                o = psum[:, JOB[name] % 4, 0:2 * n].rearrange("p (m c) -> p m c", c=2)
                v.tensor_tensor(ada[:, first:first + n, :], o, spread(col("b_ada", first, n), 2, 2), ALU.add) \
                    .then_inc(drain(name), 1)
                wait_drained(dve, name)

            take_modulation("ada_a", 0, 16, 4)
            v.scalar_tensor_tensor(out=mod1, in0=ada[:, 8:16, :], scalar=1.0, in1=spread(col("g1", 0, KD), 2, 2),
                                   op0=ALU.add, op1=ALU.mult).then_inc(s_mod1, 1)
            dve.wait_ge(s_mod1, 1)
            for k in range(1, KD, 2):
                o = take(dve, f"xt{k}")
                v.tensor_scalar(h1T[:, k, 0:NLAT], o[:, 0:NLAT], mod1[:, k, 0:1], ada[:, k, 0:1], ALU.mult, ALU.add)
                v.tensor_scalar(h1T[:, k, NLAT:NT], o[:, NLAT:NT], mod1[:, k, 1:2], ada[:, k, 1:2],
                                ALU.mult, ALU.add).then_inc(drain(f"xt{k}"), 1)

            def conv(src, width, taps, w, dst, lat, cx, done):
                n = width - taps + 1
                step(v.tensor_scalar(convt[:, 0:n], src[:, 0:n], w(0), None, ALU.mult))
                for k in range(1, taps - 1):
                    step(v.scalar_tensor_tensor(out=convt[:, 0:n], in0=src[:, k:k + n], scalar=w(k),
                                                in1=convt[:, 0:n], op0=ALU.mult, op1=ALU.add))
                k = taps - 1
                v.scalar_tensor_tensor(out=dst[:, 0:NLAT], in0=src[:, k:k + NLAT], scalar=w(k),
                                       in1=convt[:, 0:NLAT], op0=ALU.mult, op1=ALU.add)
                at = cx - lat
                v.scalar_tensor_tensor(out=dst[:, NLAT:NT], in0=src[:, at + k:at + k + NCTX], scalar=w(k),
                                       in1=convt[:, at:at + NCTX], op0=ALU.mult, op1=ALU.add).then_inc(done, 1)

            for j in range(2):
                wait_drained(dve, f"xl{j}")
                conv(xl_pad[:, j, :], XW, 4, lambda k: col("conv", 2 * k + j), xc[:, j, :], XLAT, XCTX, s_xc)
                dve.wait_ge(s_xc, j + 1)
            for j in range(2):
                o = take(dve, f"xs{j}")
                wait_drained(dve, f"c{j}")
                v.tensor_tensor(cs_pad[:, j, SLAT:SLAT + NLAT], o[:, 0:NLAT], c_sb[:, j, 0:NLAT], ALU.mult)
                v.tensor_tensor(cs_pad[:, j, SCTX:SCTX + NCTX], o[:, NLAT:NT], c_sb[:, j, NLAT:NT], ALU.mult) \
                    .then_inc(drain(f"xs{j}"), 1)
            for j in range(2):
                wait_drained(dve, f"xs{j}")
                conv(cs_pad[:, j, :], SW, 3, lambda k: col("sc", 2 * k + j), ys[:, j, :], SLAT, SCTX, s_ysc)
                dve.wait_ge(s_ysc, j + 1)
            for j in range(2):
                wait_drained(dve, f"gl{j}")
                step(v.tensor_scalar(yf[:, j, :], yf[:, j, :], GELU_A, 1.0, ALU.mult, ALU.add))
                v.tensor_tensor(yf[:, j, :], yf[:, j, :], gl[:, j, :], ALU.mult).then_inc(s_gpoly, 1)

            def lru_dve(n):
                d, j = divmod(n, 2)
                dve.wait_ge(s_lact, 2 * n + 1)
                v.scalar_tensor_tensor(out=lt[:, 3, :], in0=lt[:, 3, :], scalar=1.0, in1=lt[:, 0, :],
                                       op0=ALU.add, op1=ALU.mult).then_inc(s_ldve, 1)
                step(v.scalar_tensor_tensor(out=lt[:, 1, :], in0=lt[:, 1, :], scalar=1.0, in1=xc[:, j, :],
                                            op0=ALU.add, op1=ALU.mult))
                dve.wait_ge(s_lact, 2 * n + 2)
                step(v.tensor_tensor(lt[:, 1, :], lt[:, 1, :], lt[:, 3, :], ALU.mult))
                av, bv, h0 = lt[:, 2, :], lt[:, 1, :], col("h0", n)
                if d == 0:
                    v.tensor_tensor_scan(yl[:, j, 0:NLAT], av[:, 0:NLAT], bv[:, 0:NLAT], h0, ALU.mult, ALU.add)
                    v.tensor_tensor_scan(yl[:, j, NLAT:NT], av[:, NLAT:NT], bv[:, NLAT:NT], 0.0, ALU.mult, ALU.add) \
                        .then_inc(s_ldve, 1)
                    dve.wait_ge(s_ldve, 3 * n + 2)
                    v.tensor_copy(tiny("fin", n, 1), yl[:, j, NT - 1:NT]).then_inc(s_fin, 1)
                    dve.wait_ge(s_fin, n + 1)
                    dve.sem_inc(s_ldve, 1)
                else:
                    hv = lt[:, 3, :]
                    v.tensor_tensor_scan(hv[:, NLAT - 1::-1], av[:, NLAT - 1::-1], bv[:, NLAT - 1::-1], h0,
                                         ALU.mult, ALU.add)
                    v.tensor_tensor_scan(hv[:, NT - 1:NLAT - 1:-1], av[:, NT - 1:NLAT - 1:-1],
                                         bv[:, NT - 1:NLAT - 1:-1], 0.0, ALU.mult, ALU.add).then_inc(s_ldve, 1)
                    dve.wait_ge(s_ldve, 3 * n + 2)
                    v.tensor_copy(tiny("fin", n, 1), hv[:, NLAT:NLAT + 1]).then_inc(s_fin, 1)
                    step(v.tensor_tensor(yl[:, j, :], yl[:, j, :], hv, ALU.add))
                    dve.wait_ge(s_fin, n + 1)
                    dve.sem_inc(s_ldve, 1)
                    v.scalar_tensor_tensor(out=yl[:, j, :], in0=yl[:, j, :], scalar=0.5, in1=gl[:, j, :],
                                           op0=ALU.mult, op1=ALU.mult).then_inc(s_yl, 1)

            lru_dve(0)
            for j in range(2):
                dve.wait_ge(s_gtanh, j + 1)
                v.scalar_tensor_tensor(out=gl[:, j, :], in0=yf[:, j, :], scalar=1.0, in1=gl[:, j, :],
                                       op0=ALU.add, op1=ALU.mult).then_inc(s_gelu, 1)
            lru_dve(1)
            dve.wait_ge(s_gelu, 2)
            lru_dve(2)
            lru_dve(3)

            dve.wait_ge(s_yzero, 16)
            for t in range(TT):
                o = take(dve, f"fa{t}")
                v.tensor_copy(af[:, t, :], o[:, 0:512]).then_inc(drain(f"fa{t}"), 1)
            for j in range(2):
                o = take(dve, f"fy{j}")
                v.tensor_copy(yf[:, j, :], o[:, 0:NT]).then_inc(drain(f"fy{j}"), 1)

            def latents(t):
                o = take(dve, f"qkv{t}")
                dve.wait_ge(s_ssq, t + 1)
                v.tensor_copy(qkv_tok[:, t, :], o[:, 0:QKV]).then_inc(drain(f"qkv{t}"), 1)
                dve.wait_ge(s_rq, t + 1)
                wait_drained(dve, f"qkv{t}")
                v.tensor_scalar(qkv_tok[:, t, 0:QL], qkv_tok[:, t, 0:QL], ssq[:, t, 0:1], None, ALU.mult)
                v.tensor_scalar(qkv_tok[:, t, QL:QL + KVL], qkv_tok[:, t, QL:QL + KVL], ssq[:, t, 1:2], None,
                                ALU.mult)
                v.tensor_copy(kr_tok[:, t, :], qkv_tok[:, t, QL + KVL:QKV]).then_inc(s_qn, 1)

            def take_latents(t):
                o = take(dve, f"ct{t}")[:, 0:CT * P].rearrange("p (i n) -> p i n", i=CT)
                v.tensor_tensor(qcT[:, :, t * P:(t + 1) * P], o[:, 0:3, :], spread(col("g_qa", 0, 3), 2, P), ALU.mult)
                v.tensor_tensor(ckvT[:, :, t * P:(t + 1) * P], o[:, 3:CT, :], spread(col("g_kva", 0, 2), 2, P),
                                ALU.mult).then_inc(drain(f"ct{t}"), 1)

            latents(0)
            for t in range(1, TT):
                latents(t)
                take_latents(t - 1)
            take_latents(TT - 1)
            dve.wait_ge(s_ksq, 1)
            step(v.tensor_reduce(tiny("sskr"), rot.rearrange("p a n -> p (a n)")[:, 0:KT * ROPE]
                                 .rearrange("p (t n) -> p t n", n=ROPE), AX.X, ALU.add))
            v.tensor_scalar(tiny("sskr"), tiny("sskr"), 1.0 / QK, EPS, ALU.mult, ALU.add).then_inc(s_ksq, 1)
            dve.wait_ge(s_ksq, 2)

            take_modulation("ada_b", 16, 32, ADA_CHUNKS)
            for i in range(2):
                for w, at_ in ((0, 16), (6, 40)):
                    v.tensor_scalar(rowsrc[:, w + i, :], ada[:, at_:at_ + KD, i], 0.5, None, ALU.mult)
                v.scalar_tensor_tensor(out=rowsrc[:, 2 + i, :], in0=ada[:, 32:40, i], scalar=1.0,
                                       in1=col("g2", 0, KD), op0=ALU.add, op1=ALU.mult)
                ins = v.tensor_copy(rowsrc[:, 4 + i, :], ada[:, 24:32, i])
            ins.then_inc(s_mod1, 1)
            o = take(dve, "rt")
            v.tensor_copy(rowsT[0:8 * KD, :], o[0:8 * KD, 0:P]).then_inc(drain("rt"), 1)
            wait_drained(dve, "rt")
            dve.sem_inc(s_rowsT, 1)

            def keys_dve(t):
                o, b = take(dve, f"vk{t}"), t % 2
                if t >= 2:
                    dve.wait_ge(filled, filled_count(f"kt{t - 2}"))
                dve.wait_ge(s_kss, t + 1)
                v.tensor_copy(tokbuf[:, b, :, 0:NOPE], o[:, 0:512].rearrange("p (h n) -> p h n", h=H)) \
                    .then_inc(drain(f"vk{t}"), 1)
                step(v.tensor_reduce(rs[:, b, :], sqbuf[:, 0:512].rearrange("p (h n) -> p h n", h=H), AX.X, ALU.add))
                v.tensor_scalar(rs[:, b, :], rs[:, b, :], 1.0 / QK, tiny("sskr", t, 1), ALU.mult, ALU.add) \
                    .then_inc(s_krs, 1)
                dve.wait_ge(s_hr, t + 1)
                wait_drained(dve, f"vk{t}")
                v.tensor_tensor(tokbuf[:, b, :, 0:NOPE], tokbuf[:, b, :, 0:NOPE], spread(rs[:, b, :], 2, NOPE),
                                ALU.mult)
                dve.wait_ge(s_krr, 1)
                v.tensor_tensor(tokbuf[:, b, :, NOPE:QK], spread(kr_rot[:, t, :], 1, H), spread(rs[:, b, :], 2, ROPE),
                                ALU.mult).then_inc(s_tok, 1)

            def queries_dve(t):
                n = KT + t
                o, b = take(dve, f"q{t}"), n % 2
                dve.wait_ge(filled, filled_count(f"kt{n - 2}" if n - 2 < KT else f"qt{n - 2 - KT}"))
                dve.wait_ge(s_kss, n + 1)
                v.tensor_copy(tokbuf[:, b, :, :], o[:, 0:H * QK].rearrange("p (h n) -> p h n", h=H)) \
                    .then_inc(drain(f"q{t}"), 1)
                step(v.tensor_reduce(rs[:, b, :], sqbuf[:, :].rearrange("p (h n) -> p h n", h=H), AX.X, ALU.add))
                v.tensor_scalar(rs[:, b, :], rs[:, b, :], 1.0 / QK, EPS, ALU.mult, ALU.add).then_inc(s_krs, 1)
                dve.wait_ge(s_hr, n + 1)
                wait_drained(dve, f"q{t}")
                v.tensor_tensor(tokbuf[:, b, :, :], tokbuf[:, b, :, :], spread(rs[:, b, :], 2, QK), ALU.mult) \
                    .then_inc(s_qsc, 1)

            def take_queries(t):
                o = take(dve, f"qt{t}")
                v.tensor_scalar(qT[0:QK, :, t * P:(t + 1) * P], o[0:QK, :].rearrange("p (h n) -> p h n", h=H),
                                tiny("gcol")[0:QK, :], None, ALU.mult).then_inc(drain(f"qt{t}"), 1)

            for t in range(KT):
                keys_dve(t)
            queries_dve(0)
            for t in range(1, TT):
                queries_dve(t)
                take_queries(t - 1)
            take_queries(TT - 1)

            def maxima(i):
                w = NT if UNITS[i][1] < LT else P
                dve.wait_ge(s_S, i + 1)
                step(v.tensor_reduce(tiny("mx", i % 2, 1), psum[:, i % 2, 0:w], AX.X, ALU.max))
                v.tensor_scalar(tiny("nmx", i % 2, 1), tiny("mx", i % 2, 1), -ATTN_SCALE, None, ALU.mult) \
                    .then_inc(s_nmx, 1)

            maxima(0)
            maxima(1)
            for i, (h, t) in enumerate(UNITS):
                if i % 2 == 0:
                    w = NT if t < LT else P
                    dve.wait_ge(s_T, i + 1)
                    if i >= 2:
                        dve.wait_ge(s_V, i - 1)
                    v.tensor_copy(probT[:, 0, 0:w], psum[:, 2, 0:w]).then_inc(s_pT, 1)
                if i + 2 < len(UNITS):
                    maxima(i + 2)
                dve.wait_ge(s_prob, i + 1)
                step(v.reciprocal(tiny("rinv", i % 2, 1), tiny("rsum", i % 2, 1)))
                dve.wait_ge(s_V, i + 1)
                v.tensor_scalar(o_tok[:, t, h * VD:(h + 1) * VD], psum[:, 3, (i % 2) * 512:(i % 2) * 512 + VD],
                                tiny("rinv", i % 2, 1), None, ALU.mult).then_inc(s_o, 1)
            for p in (1, 3):
                dve.wait_ge(s_oT, p + 1)
                v.tensor_copy(oT[:, p, :], psum[:, p, 0:NT]).then_inc(s_oTd, 1)

            dve.sem_inc(s_mrg, 2)
            with dve.Fori(0, KD - 1, 2) as m:
                for g in range(8):
                    s, b = divmod(g, 4)
                    dve.wait_ge(s_gth, m * 4 + (g + 3))
                    dve.wait_ge(s_R, m * 4 + (g + 1))
                    v.scalar_tensor_tensor(out=acc if b == 0 else gtmp, in0=gth[:, g % 2, :], scalar=1.0,
                                           in1=psum[:, (2 * g + 1) % 4, 0:NT], op0=ALU.add, op1=ALU.mult) \
                        .then_inc(s_mrg, 1)
                    if b == 0:
                        continue
                    dve.wait_ge(s_mrg, m * 4 + (g + 3))
                    if b < 3:
                        v.tensor_tensor(acc, acc, gtmp, ALU.add).then_inc(s_add, 1)
                        dve.wait_ge(s_add, m * 2 + (2 * s + b))
                    else:
                        v.tensor_tensor(merged[:, bass.ds(m + s, 1), :].rearrange("p a n -> p (a n)"), acc, gtmp,
                                        ALU.add).then_inc(s_mdone, 1)
                        dve.wait_ge(s_mdone, m + (s + 1))

            dve.wait_ge(loaded["xres"], 16)
            dve.wait_ge(loaded["g1r"], 16)

            def residual(t):
                k = 0 if t < LT else 1
                dve.wait_ge(s_wo, t + 1)
                if t:
                    dve.wait_ge(s_x1, t)
                step(v.tensor_tensor(wide2, psum[:, t % 2, :], g1_row[:, k, :], ALU.mult))
                v.tensor_tensor(x1[:, t, :], x1[:, t, :], wide2, ALU.add).then_inc(s_x1, 1)

            def modulated(t):
                k = 0 if t < LT else 1
                dve.wait_ge(s_r2, t + 1)
                step(v.scalar_tensor_tensor(out=h2[:, t, :], in0=x1[:, t, :], scalar=tiny("ss2", t, 1),
                                            in1=a2_row[:, k, :], op0=ALU.mult, op1=ALU.mult))
                v.tensor_tensor(h2[:, t, :], h2[:, t, :], b2_row[:, k, :], ALU.add).then_inc(s_h2, 1)

            wide2 = view(r_y, 2 * D, D)
            for t in range(TT):
                residual(t)
            dve.wait_ge(loaded["a2r"], 16)
            dve.wait_ge(loaded["b2r"], 16)
            dve.wait_ge(s_wo, TT)
            for t in range(TT):
                modulated(t)

            lg = r3("lg", LOGITS)
            dve.wait_ge(s_lg, 1)
            dve.wait_ge(loaded["rows"], 16)
            step(v.tensor_tensor(lg, psum[:, 0, 0:TT * LOGITS].rearrange("p (t n) -> p t n", n=LOGITS),
                                 spread(row("br"), 1, TT), ALU.add))

            def first_of_max(x, n, m, eq, hot, rev):
                step(v.tensor_tensor(eq, x, spread(m, 2, n), ALU.is_equal))
                step(v.tensor_tensor(eq, eq, spread(const(rev), 1, TT), ALU.mult))
                step(v.tensor_reduce(r("mm"), eq, AX.X, ALU.max))
                step(v.tensor_tensor(hot, eq, spread(r("mm"), 2, n), ALU.is_equal))

            step(v.tensor_reduce(r("gmax"), lg[:, :, 0:NG], AX.X, ALU.max))
            v.tensor_tensor(r3("e4", NG), lg[:, :, 0:NG], spread(r("gmax"), 2, NG), ALU.subtract).then_inc(s_rexp, 1)
            first_of_max(lg[:, :, 0:NG], NG, r("gmax"), r3("q4", NG), r3("og", NG), "rev4")
            dve.wait_ge(s_ract, 1)
            step(v.tensor_reduce(r("gw"), r3("e4", NG), AX.X, ALU.add))
            step(v.reciprocal(r("gw"), r("gw")))
            for g in range(NG):
                v.tensor_tensor(r3("mul", NE)[:, :, g * NE8:(g + 1) * NE8], lg[:, :, NG + g * NE8:NG + (g + 1) * NE8],
                                spread(r3("og", NG)[:, :, g], 2, NE8), ALU.mult).then_inc(s_part, 1)
            dve.wait_ge(s_part, NG)
            step(v.tensor_tensor(r3("ein", NE8), r3("mul", NE)[:, :, 0:NE8], r3("mul", NE)[:, :, NE8:2 * NE8],
                                 ALU.add))
            for g in range(2, NG):
                step(v.tensor_tensor(r3("ein", NE8), r3("ein", NE8), r3("mul", NE)[:, :, g * NE8:(g + 1) * NE8],
                                     ALU.add))
            step(v.tensor_reduce(r("v1"), r3("ein", NE8), AX.X, ALU.max))
            first_of_max(r3("ein", NE8), NE8, r("v1"), r3("q8", NE8), r3("o1", NE8), "rev8")
            step(v.scalar_tensor_tensor(out=r("ein"), in0=r("o1"), scalar=-BIG, in1=r("ein"), op0=ALU.mult,
                                        op1=ALU.add))
            step(v.tensor_reduce(r("v2"), r3("ein", NE8), AX.X, ALU.max))
            first_of_max(r3("ein", NE8), NE8, r("v2"), r3("q8", NE8), r3("o2", NE8), "rev8")
            v.tensor_tensor(r("ed"), r("v2"), r("v1"), ALU.subtract).then_inc(s_rexp, 1)
            for g in range(NG):
                gg = spread(r3("og", NG)[:, :, g], 2, NE8)
                v.tensor_tensor(r3("m1", NE)[:, :, g * NE8:(g + 1) * NE8], r3("o1", NE8), gg, ALU.mult)
                v.tensor_tensor(r3("m2", NE)[:, :, g * NE8:(g + 1) * NE8], r3("o2", NE8), gg, ALU.mult) \
                    .then_inc(s_part, 1)
            dve.wait_ge(s_part, 2 * NG)
            v.tensor_tensor(r("msum"), r("m1"), r("m2"), ALU.add).then_inc(s_onehot, 1)
            dve.wait_ge(s_ract, 2)
            step(v.tensor_scalar(r("v1"), r("ed"), 1.0, None, ALU.add))
            step(v.reciprocal(r("v1"), r("v1")))
            step(v.tensor_tensor(tiny("wt", 0, TT), r("v1"), r("gw"), ALU.mult))
            step(v.tensor_tensor(tiny("wt", TT, TT), tiny("wt", 0, TT), r("ed"), ALU.mult))
            v.memset(r("one"), 1.0)
            dve.wait_ge(s_pre, 1)
            step(v.tensor_copy(r("pre"), psum[:, 1, 0:TT * NE]))
            step(v.tensor_copy(r("n"), psum[:, 1, TT * NE:(TT + 1) * NE]))
            step(v.tensor_scalar(r("ovn"), r("n"), float(C), None, ALU.is_gt))
            for j in range(2, (NT - 1) // C + 1):
                step(v.scalar_tensor_tensor(out=r("ovn"), in0=r("n"), scalar=float(j * C), in1=r("ovn"),
                                            op0=ALU.is_gt, op1=ALU.add))
            step(v.tensor_tensor_scan(r("incl"), r("one"), r("ovn"), 0.0, ALU.mult, ALU.add))
            step(v.tensor_tensor(r("db"), r("incl"), r("ovn"), ALU.subtract))
            step(v.tensor_scalar(r("db"), r("db"), float(C), float((NE - 1) * C), ALU.mult, ALU.add))
            step(v.tensor_tensor(r("db"), r("db"), const("ebase"), ALU.subtract))
            step(v.tensor_scalar(r("t3"), r("pre"), float(C), None, ALU.is_ge))
            step(v.tensor_tensor(r3("t3", NE), r3("t3", NE), spread(r("db"), 1, TT), ALU.mult))
            step(v.tensor_tensor(r("t3"), r("t3"), r("pre"), ALU.add))
            step(v.tensor_tensor(r3("t3", NE), r3("t3", NE), spread(const("ebase"), 1, TT), ALU.add))
            for i, m in enumerate(("m1", "m2")):
                step(v.tensor_tensor(r("mul"), r("t3"), r(m), ALU.mult))
                step(v.tensor_reduce(r("sl"), r3("mul", NE), AX.X, ALU.add))
                step(v.tensor_copy(slots[:, i * TT:(i + 1) * TT], r("sl")))
            v.tensor_copy(tok_id[:, :], const("tok")).then_inc(s_slot, 1)
            step(v.tensor_tensor(r3("cmp", NE), spread(r("incl"), 1, NX),
                                 spread(const("xio"), 2, NE), ALU.is_le))
            step(v.tensor_reduce(r("xe"), r3("cmp", NE), AX.X, ALU.add))
            step(v.tensor_scalar(r("xe"), r("xe"), float(NE - 1), None, ALU.min))
            step(v.tensor_copy(xinfo[:, 0:NX], r("xe")))
            v.tensor_copy(xinfo[:, NX:NX + 1], r("incl")[:, NE - 1:NE]).then_inc(s_slot, 1)

            def gate(tanh, n_t, gated, n_g, hs, done):
                dve.wait_ge(tanh, n_t)
                a_, u_ = (psum[:, 1, i * 2 * C:(i + 1) * 2 * C].rearrange("p (f n) -> p f n", f=2) for i in range(2))
                v.scalar_tensor_tensor(out=gate_e, in0=gate_e, scalar=1.0, in1=a_, op0=ALU.add, op1=ALU.mult) \
                    .then_inc(gated, 1)
                dve.wait_ge(gated, n_g)
                v.tensor_tensor(hT[:, hs, :, :], gate_e, u_, ALU.mult).then_inc(done, 1)

            dve.sem_inc(s_yd, 2)
            with dve.Fori(0, NE - 1, 2) as c:
                for s in range(2):
                    gate(s_eth, c + (s + 1), s_e1, c + (s + 1), s, s_hT)
                    dve.wait_ge(s_Y, c + (s + 1))
                    dve.wait_ge(y_stored[s], c * 8 + 16)
                    v.tensor_copy(y_sb[0:C, s, 512:1024], psum[0:C, 2 + s, 512:1024]).then_inc(s_yd, 1)
            n_x = dve.value_load(xinfo[0:1, NX:NX + 1], min_val=0, max_val=NX)
            with dve.Fori(0, NX) as x:
                with dve.If(x < n_x):
                    gate(x_th, x + 1, x_g, x + 1, 0, x_h)

            dve.wait_ge(loaded["g2r"], 16)
            for t in range(TT):
                b, k = t % 2, (0 if t < LT else 1)
                dve.wait_ge(yab_loaded[b], 32 * (t // 2 + 1))
                step(v.tensor_scalar(yab[:, b, 0, :], yab[:, b, 0, :], tiny("wt", t, 1), None, ALU.mult))
                step(v.scalar_tensor_tensor(out=yab[:, b, 1, :], in0=yab[:, b, 1, :], scalar=tiny("wt", TT + t, 1),
                                            in1=yab[:, b, 0, :], op0=ALU.mult, op1=ALU.add))
                step(v.tensor_tensor(yab[:, b, 1, :], yab[:, b, 1, :], g2_row[:, k, :], ALU.mult))
                v.tensor_tensor(x1[:, t, :], x1[:, t, :], yab[:, b, 1, :], ALU.add).then_inc(s_fo, 1)

        @block.gpsimd
        def _(pool):
            g = nc.gpsimd
            step = stepper(pool, pool_step)

            def rstd(x, n, done, add_eps=True):
                if add_eps:
                    step(g.tensor_scalar(x, x, EPS, None, ALU.add))
                g.tensor_tensor(x, x, tiny("mhalf", 0, n), ALU.pow).then_inc(done, 1)

            def pause(i):
                g.tensor_tensor(tiny("pause", i, 1), tiny("mhalf", 0, 1), tiny("mhalf", 0, 1), ALU.mult)

            step(g.memset(chunk_tok[:, :], 0))
            pool.dma_start(table_d.rearrange("(c p) a -> p (c a)", p=C), chunk_tok[0:C, :],
                           allow_slow_non_contiguous=True).then_inc(s_tset, 16)

            pool.wait_ge(s_set, 4)
            pool.wait_ge(s_sq1, TT)
            rstd(tiny("ss1"), TT, s_rstd1)
            step(g.memset(r_d[0:C, 0:D], 0.0))
            pool.wait_ge(s_mod1, 1)
            pool.dma_start(y_d[NE * C:SLOTS, :].rearrange("(x p) d -> p x d", p=C), spread(r_d[0:C, 0:D], 1, NX)) \
                .then_inc(s_yzero, 16)
            for j in range(2):
                wait_drained(pool, f"b{j}")
                pool.wait_ge(s_ysc, j + 1)
                g.tensor_tensor(ys[:, j, :], ys[:, j, :], b_sb[:, j, :], ALU.mult).then_inc(s_ys, 1)
            for t in range(TT):
                pool.wait_ge(s_ssq, t + 1)
                rstd(ssq[:, t, :], 2, s_rq)

            def rotate(src, dst, cos, sin, shape, m):
                tmp = [m(rot[:, i, :]) for i in range(4)]
                x1_, x2_ = src
                g.tensor_tensor(tmp[0], x1_, cos, ALU.mult)
                g.tensor_tensor(tmp[1], x2_, sin, ALU.mult)
                g.tensor_tensor(tmp[2], x1_, sin, ALU.mult)
                step(g.tensor_tensor(tmp[3], x2_, cos, ALU.mult))
                g.tensor_tensor(dst[0], tmp[0], tmp[1], ALU.subtract)
                return g.tensor_tensor(dst[1], tmp[2], tmp[3], ALU.add)

            pool.wait_ge(s_qn, TT)
            pool.wait_ge(loaded["krc"], 16)
            pool.wait_ge(loaded["rows"], 16)
            pool.wait_ge(loaded["consts"], 16)
            flat = rot.rearrange("p a n -> p (a n)")[:, 0:KT * ROPE].rearrange("p (t n) -> p t n", n=ROPE)
            g.tensor_tensor(flat, kr_tok, kr_tok, ALU.mult).then_inc(s_ksq, 1)
            step(g.tensor_tensor(kr_rot, kr_tok, spread(row("gk"), 1, KT), ALU.mult))
            pool.wait_ge(s_ksq, 2)
            cos, sin = (const(n).rearrange("p (t n) -> p t n", n=HALF) for n in ("cos", "sin"))
            halves = (kr_rot[:, 0:LT, 0:HALF], kr_rot[:, 0:LT, HALF:ROPE])
            rotate(halves, halves, cos, sin, None,
                   lambda x: x[:, 0:LT * HALF].rearrange("p (t n) -> p t n", n=HALF)).then_inc(s_krr, 1)
            for n in range(KT):
                pool.wait_ge(s_krs, n + 1)
                rstd(rs[:, n % 2, :], 8, s_hr, add_eps=False)
            for t in range(TT):
                n = KT + t
                pool.wait_ge(s_krs, n + 1)
                rstd(rs[:, n % 2, :], 8, s_hr, add_eps=False)
                pool.wait_ge(s_qsc, t + 1)
                tail = tokbuf[:, n % 2, :, NOPE:QK]
                ins = g.tensor_tensor(tail, tail, spread(row("gq"), 1, H), ALU.mult)
                if t < LT:
                    step(ins)
                    halves = (tail[:, :, 0:HALF], tail[:, :, HALF:ROPE])
                    ins = rotate(halves, halves, spread(cos[:, t, :], 1, H), spread(sin[:, t, :], 1, H), None,
                                 lambda x: x.rearrange("p (h n) -> p h n", h=H))
                ins.then_inc(s_tok, 1)

            for t in range(TT):
                pool.wait_ge(s_sq2, t + 1)
                rstd(tiny("ss2", t, 1), 1, s_r2)
            pool.wait_ge(s_tset, 16)
            pool.wait_ge(s_slot, 1)
            for i in range(2):
                for t in range(TT):
                    pool.indirect_dma_start(table_d, bass.IndirectOffsetOnAxis(ap=slots[:, i * TT + t:i * TT + t + 1],
                                                                              axis=0),
                                            tok_id[:, t:t + 1], None).then_inc(s_scat, 16)
            def gather(dst, idx, done):
                pool.indirect_dma_start(dst, None, h2_d, bass.IndirectOffsetOnAxis(ap=idx, axis=0)).then_inc(done, 16)

            pool.wait_ge(s_h2d, 16 * TT)
            pool.wait_ge(s_tab[0], 16)
            for c in range(2):
                gather(xg[0:C, c, :], chunk_tok[0:C, c:c + 1], xg_loaded[c])
            pool.wait_ge(s_tab[1], 16)

            def step_in_loop(ins, n, s):
                ins.then_inc(s_now, 1)
                pool.wait_ge(s_now, n)
                pause(s)

            with pool.Fori(2, NE - 1, 2) as c:
                for s in range(2):
                    pool.wait_ge(s_xT, c + (s - 1))
                    step_in_loop(g.tensor_copy(now_tok[s][0:C, :], chunk_tok[0:C, bass.ds(c + s, 1)]), c + (s - 1),
                                 s)
                    gather(xg[0:C, s, :], now_tok[s][0:C, :], xg_loaded[s])
            pool.wait_ge(s_xT, NE - 1)
            gather(xg[0:C, 0, :], chunk_tok[0:C, NE:NE + 1], xg_loaded[0])
            pool.wait_ge(s_xT, NE + 1)
            n_x = pool.value_load(xinfo[0:1, NX:NX + 1], min_val=0, max_val=NX)
            with pool.Fori(0, NX) as x:
                with pool.If(x < n_x):
                    pool.wait_ge(x_idx, (x + 1) * 16)
                    pause(2)
                    gather(xg[0:C, 0, :], xtok_id[0:C, :], x_in)
            for s in range(2):
                pool.wait_ge(y_stored[s], 8 * NE + 16)
            pool.wait_ge(x_st, n_x * 16 + 16)
            pause(3)
            for t in range(TT):
                if t >= 2:
                    pool.wait_ge(s_fo, t - 1)
                for i in range(2):
                    pool.indirect_dma_start(yab[:, t % 2, i, :], None, y_d, bass.IndirectOffsetOnAxis(
                        ap=slots[:, i * TT + t:i * TT + t + 1], axis=0)).then_inc(yab_loaded[t % 2], 16)


def _tiles(w, n):
    k = w.shape[0] // P
    return w.reshape(k, P, -1).transpose(1, 0, 2).reshape(P, -1) if n is None else \
        w.reshape(k, P, -1, n).transpose(2, 1, 0, 3).reshape(-1, P, k * n)


def _columns_of(v):
    return v.reshape(-1, P).T


def _constants():
    t = np.arange(NLAT)
    inv = 10000.0 ** (-np.arange(HALF // 2) / (HALF // 2))
    ang = np.concatenate([(t // GRID_W)[:, None] * inv, (t % GRID_W)[:, None] * inv], axis=1)
    ang = ang.reshape(LT, P, HALF).transpose(1, 0, 2).reshape(P, -1)
    c64 = 2 * np.pi * (np.outer(np.arange(64), np.arange(64)) % 64) / 64
    two = np.eye(2)
    n = np.arange(NCTX)
    dc = 2 * np.pi * (np.outer(n, n) % NCTX) / NCTX
    one = np.ones((P, 1))
    parts = {
        "ident": np.eye(P), "tri": np.triu(np.ones((P, P)), 1), "cos": np.cos(ang), "sin": np.sin(ang),
        "rev4": one * np.arange(NG, 0, -1), "rev8": one * np.arange(NE8, 0, -1), "ebase": one * np.arange(NE) * C,
        "xio": one * np.arange(NX), "tok": np.arange(NT).reshape(TT, P).T,
        "cs64": np.concatenate([np.kron(two, np.cos(c64)), np.kron(two, np.sin(c64))], axis=1),
        "dftc": np.concatenate([np.cos(dc), -np.sin(dc)], axis=1) / np.sqrt(NCTX * 64.0),
    }
    consts = np.concatenate([parts[k] for k in CONST], axis=1).astype(np.float32)
    dl = 2 * np.pi * (np.outer(t, t) % NLAT) / NLAT
    dft = np.stack([np.cos(dl), -np.sin(dl)], axis=1) / np.sqrt(NLAT * 64.0)
    dft = dft.reshape(LT, P, 2 * NLAT).transpose(1, 0, 2).reshape(P, -1).astype(np.float32)
    return consts, dft


def kernel(x_prompt, x_sample, cache_ckv, cache_krope, state_rglru, c, c_ctx,
           norm1_g, norm2_g, w_ada, b_ada, w_in, lru_conv, lru_wa, lru_ba, lru_wx, lru_bx,
           lru_lam, sc_conv, g_qa, w_qb, g_kva, w_kvb, g_qn, g_kn, w_pf, w_pl, w_ps, w_pm,
           w_gate, w_out, w_gr, b_gr, w_er, b_er, w1, w3, w2):
    from concourse import bacc
    from concourse.bass_utils import run_bass_kernel_spmd

    f = lambda v: np.asarray(v)
    cat = np.concatenate
    consts, dft = _constants()
    win = f(w_in)[0]
    uf, xl, glu, b, cc, xs = (win[:, i * 256:(i + 1) * 256] for i in range(6))
    zcols = cat([xl, cc, xs, glu, b, uf], axis=1)
    qkv = win[:, 6 * 256:]
    pad = lambda v: cat([v, np.zeros(P - QK, v.dtype)])[:, None]
    lruw = np.zeros((P, 2, 2, 2, P), np.float32)
    for x, w in enumerate((f(lru_wa)[0], f(lru_wx)[0])):
        for j in range(2):
            for i in range(2):
                lruw[i * 64:(i + 1) * 64, :, x, j, i * 64:(i + 1) * 64] = w[:, 2 * j + i].transpose(1, 0, 2)
    vcols = {
        "b_ada": _columns_of(f(b_ada)[0]), "g1": _columns_of(f(norm1_g)[0]), "g2": _columns_of(f(norm2_g)[0]),
        "conv": _columns_of(f(lru_conv)[0]), "sc": _columns_of(f(sc_conv)[0]), "ba": _columns_of(f(lru_ba)[0]),
        "bx": _columns_of(f(lru_bx)[0]), "lam": _columns_of(f(lru_lam)[0]), "g_qa": _columns_of(f(g_qa)[0]),
        "g_kva": _columns_of(f(g_kva)[0]), "h0": _columns_of(f(state_rglru)[0, 0]),
        "gq": pad(f(g_qn)[0]), "gk": pad(f(g_kn)[0]),
    }
    vrows = {"gk": f(g_kn)[0, NOPE:], "gq": f(g_qn)[0, NOPE:], "br": cat([f(b_gr)[0], f(b_er)[0]])}
    wkvb = f(w_kvb)[0]
    gate = f(w_gate)[0].reshape(KD, P, 4, KD, P)
    wbr = cat([f(w)[0] for w in (w_pf, w_pl, w_ps, w_pm)], axis=0)
    w13 = cat([f(w1)[0], f(w3)[0]], axis=2).reshape(NE, KD, P, 2 * FE).transpose(0, 2, 1, 3).reshape(NE, P, -1)
    w2t = f(w2)[0].reshape(NE, 2, P, D).transpose(0, 2, 1, 3).reshape(NE, P, -1)
    arrays = {
        "x": cat([f(x_sample)[0], f(x_prompt)[0]], axis=0),
        "cond": np.stack([_columns_of(f(c)[0]), _columns_of(f(c_ctx))], axis=2).reshape(P, -1),
        "cols": cat([vcols[k] for k in COLS], axis=1),
        "rows": np.tile(cat([vrows[k] for k in ROWS]), (P, 1)),
        "consts": consts, "dft": dft,
        "lruw": lruw.reshape(P, -1),
        "ckv_cache": _tiles(f(cache_ckv)[0, 0].T, None),
        "kr_cache": f(cache_krope)[0, 0],
        "w_r": _tiles(cat([f(w_gr)[0], f(w_er)[0]], axis=1), None),
        "w_ada": _tiles(f(w_ada)[0], 512),
        "w_in": _tiles(zcols, P).reshape(3, 4, P, D).transpose(0, 2, 1, 3).reshape(3, P, 4 * D),
        "w_qkv": qkv.reshape(2, 4, P, QKV).transpose(0, 2, 1, 3).reshape(2, P, 4 * QKV),
        "w_kv": _tiles(cat([wkvb[:, :, :NOPE].reshape(KVL, -1), wkvb[:, :, NOPE:].reshape(KVL, -1)], axis=1), None),
        "w_q": _tiles(f(w_qb)[0].reshape(QL, -1), None),
        "w_gate": gate.transpose(3, 1, 2, 0, 4).reshape(KD, P, 4 * D),
        "w_br": _tiles(wbr, P),
        "w_out": f(w_out)[0].reshape(2, 4, P, D).transpose(0, 2, 1, 3).reshape(2, P, 4 * D),
        "w_e": cat([w13, w2t], axis=2),
    }
    outputs = {"y": [NT, D], "ckv": [P, 2 * NCTX], "krope": [NCTX, ROPE], "rglru": [P, 4]}
    nc = bacc.Bacc("TRN2", target_bir_lowering=False, num_devices=1)
    ins, given = {}, {}
    for name, v in arrays.items():
        v = np.ascontiguousarray(v)
        given[f"in_{name}"] = v
        ins[name] = nc.dram_tensor(f"in_{name}", list(v.shape), F32, kind="ExternalInput").ap()
    outs = {n: nc.dram_tensor(f"out_{n}", s, F32, kind="ExternalOutput").ap() for n, s in outputs.items()}
    build(nc, ins, outs)
    got = run_bass_kernel_spmd(nc, [given], core_ids=[0]).results[0]
    y = got["out_y"]
    ckv = got["out_ckv"].reshape(P, 2, NCTX).transpose(2, 1, 0).reshape(1, 1, NCTX, KVL)
    lru = got["out_rglru"].T.reshape(1, 1, 2, 256)
    return (y[NLAT:][None], y[:NLAT][None], ckv, got["out_krope"][None, None], lru)
```
